# Optimizing a Trainium2 kernel written in Bass

```python
import jax, jax.numpy as jnp
from jax import lax
import numpy as np

D_MODEL = 2048
BATCH = 1
SEQ = 256
DEPTH = 1

HEAD_DIM = 128
EPS = 1e-6
GDN_HEADS = 8
GDN_WIDTH = GDN_HEADS * HEAD_DIM
GDN_CONV = 4
GDN_CHUNK = 64
SWA_GROUPS = ((128, 1), (512, 4), (2048, 16))
SWA_HEADS_PER_GROUP = 4
SWA_HEADS = SWA_HEADS_PER_GROUP * len(SWA_GROUPS)
SWA_WIDTH = SWA_HEADS * HEAD_DIM
SWA_OUT_WIDTH = SWA_HEADS_PER_GROUP * HEAD_DIM
SWA_BLOCK = 128
ROPE_THETA = 10000.0
NEG_INF = -1e30
D_FF = 4 * D_MODEL
IN_SIZES = (3 * GDN_WIDTH, GDN_WIDTH, GDN_HEADS, GDN_HEADS, 3 * SWA_WIDTH, D_MODEL, D_MODEL)
IN_COLS = sum(IN_SIZES)

kernel_name = "hybrid_gdn_dilated_swa_block"

def _rmsnorm(x, w):
    x32 = x.astype(jnp.float32)
    y = x32 * lax.rsqrt(jnp.mean(jnp.square(x32), axis=-1, keepdims=True) + EPS)
    return (y * w.astype(jnp.float32)).astype(x.dtype)

def _l2norm(x):
    x32 = x.astype(jnp.float32)
    return x32 * lax.rsqrt(jnp.sum(jnp.square(x32), axis=-1, keepdims=True) + EPS)

def _split_cols(t):
    points, acc = [], 0
    for sz in IN_SIZES[:-1]:
        acc += sz
        points.append(acc)
    return jnp.split(t, points, axis=-1)

def _causal_conv(x, w):
    c = x.shape[-1]
    return lax.conv_general_dilated(
        x, w[:, None, :].astype(x.dtype), window_strides=(1,),
        padding=((GDN_CONV - 1, 0),), dimension_numbers=("NWC", "WIO", "NWC"),
        feature_group_count=c)

def _rope(x, positions):
    half = HEAD_DIM // 2
    inv_freq = ROPE_THETA ** (-jnp.arange(half, dtype=jnp.float32) / half)
    ang = positions.astype(jnp.float32)[..., None] * inv_freq
    cos = jnp.concatenate([jnp.cos(ang), jnp.cos(ang)], -1)[:, :, None, :]
    sin = jnp.concatenate([jnp.sin(ang), jnp.sin(ang)], -1)[:, :, None, :]
    x32 = x.astype(jnp.float32)
    rot = jnp.concatenate([-x32[..., half:], x32[..., :half]], -1)
    return (x32 * cos + rot * sin).astype(x.dtype)

def _gdn_chunked(q, k, v, g, beta):
    b, s, h, d = q.shape
    n = s // GDN_CHUNK

    def chunks(t):
        t = t.reshape((b, n, GDN_CHUNK, h) + t.shape[3:])
        return jnp.moveaxis(t, 3, 1)

    q, k, v, g, beta = (chunks(t) for t in (q, k, v, g, beta))
    G = jnp.cumsum(g, axis=-1)
    idx = jnp.arange(GDN_CHUNK)
    incl = idx[:, None] >= idx[None, :]
    strict = idx[:, None] > idx[None, :]
    diff = G[..., :, None] - G[..., None, :]
    decay = jnp.where(incl, jnp.exp(jnp.where(incl, diff, 0.0)), 0.0)
    k_beta = k * beta[..., None]
    a_kk = jnp.where(strict, jnp.einsum("bhnid,bhnjd->bhnij", k_beta, k) * decay, 0.0)
    eye = jnp.eye(GDN_CHUNK, dtype=q.dtype)
    rhs = jnp.concatenate([v * beta[..., None], k_beta * jnp.exp(G)[..., None]], axis=-1)
    sol = lax.linalg.triangular_solve(eye + a_kk, rhs, left_side=True, lower=True,
                                      unit_diagonal=True)
    u, w = sol[..., :d], sol[..., d:]
    a_qk = jnp.where(incl, jnp.einsum("bhnid,bhnjd->bhnij", q, k) * decay, 0.0)
    q_dec = q * jnp.exp(G)[..., None]
    g_last = G[..., -1]
    k_dec = k * jnp.exp(g_last[..., None] - G)[..., None]

    def step(state, inp):
        u_c, w_c, qd_c, aqk_c, kd_c, gl_c = inp
        v_new = u_c - jnp.einsum("bhcd,bhde->bhce", w_c, state)
        o_c = (jnp.einsum("bhcd,bhde->bhce", qd_c, state)
               + jnp.einsum("bhij,bhje->bhie", aqk_c, v_new))
        state = (state * jnp.exp(gl_c)[..., None, None]
                 + jnp.einsum("bhcd,bhce->bhde", kd_c, v_new))
        return state, o_c

    xs = tuple(jnp.moveaxis(t, 2, 0) for t in (u, w, q_dec, a_qk, k_dec, g_last))
    state0 = jnp.zeros((b, h, d, v.shape[-1]), q.dtype)
    _, o = lax.scan(step, state0, xs)
    o = jnp.moveaxis(o, 0, 2)
    return jnp.moveaxis(o, 1, 3).reshape(b, s, h, -1)

def _gdn_branch(qkv, z, a, bta, conv_w, a_log, dt_bias, norm_w):
    b, s, _ = qkv.shape
    qkv = jax.nn.silu(_causal_conv(qkv, conv_w))
    q, k, v = jnp.split(qkv, 3, axis=-1)
    q = _l2norm(q.reshape(b, s, GDN_HEADS, HEAD_DIM)) * (HEAD_DIM ** -0.5)
    k = _l2norm(k.reshape(b, s, GDN_HEADS, HEAD_DIM))
    v = v.reshape(b, s, GDN_HEADS, HEAD_DIM).astype(jnp.float32)
    beta = jax.nn.sigmoid(bta.astype(jnp.float32))
    g = -jnp.exp(a_log.astype(jnp.float32)) * jax.nn.softplus(
        a.astype(jnp.float32) + dt_bias.astype(jnp.float32))
    o = _gdn_chunked(q, k, v, g, beta)
    o = o * lax.rsqrt(jnp.mean(jnp.square(o), axis=-1, keepdims=True) + EPS)
    zh = z.reshape(b, s, GDN_HEADS, HEAD_DIM).astype(jnp.float32)
    o = o * norm_w.astype(jnp.float32) * jax.nn.silu(zh)
    return o.reshape(b, s, GDN_WIDTH).astype(qkv.dtype)

def _dilated_window_attention(q, k, v, n_back, dil):
    b, s, h, dh = q.shape
    L = s // dil
    nb = -(-L // SWA_BLOCK)
    Lp = nb * SWA_BLOCK

    def by_residue(t):
        t = t.reshape(b, L, dil, h, dh).transpose(0, 2, 1, 3, 4)
        t = jnp.pad(t, ((0, 0), (0, 0), (0, Lp - L), (0, 0), (0, 0)))
        return t.reshape(b, dil, nb, SWA_BLOCK, h, dh)

    def with_prev(t):
        prev = jnp.pad(t, ((0, 0), (0, 0), (1, 0), (0, 0), (0, 0), (0, 0)))[:, :, :-1]
        return jnp.concatenate([prev, t], axis=3)

    qb = by_residue(q)
    kk = with_prev(by_residue(k))
    vv = with_prev(by_residue(v))
    qi = jnp.arange(SWA_BLOCK)[:, None] + SWA_BLOCK
    kj = jnp.arange(2 * SWA_BLOCK)[None, :]
    dist = qi - kj
    blk = jnp.arange(nb)[:, None, None]
    valid = (dist >= 0) & (dist <= n_back) & ((blk - 1) * SWA_BLOCK + kj >= 0)
    scores = jnp.einsum("bdnqhc,bdnkhc->bdnhqk", qb, kk).astype(jnp.float32) * (HEAD_DIM ** -0.5)
    scores = jnp.where(valid[:, None], scores, NEG_INF)
    lse = jax.nn.logsumexp(scores, axis=-1)
    p = jnp.exp(scores - lse[..., None])
    o = jnp.einsum("bdnhqk,bdnkhc->bdnqhc", p.astype(v.dtype), vv)
    o = o.reshape(b, dil, Lp, h, dh)[:, :, :L].transpose(0, 2, 1, 3, 4).reshape(b, s, h, dh)
    lse = lse.transpose(0, 1, 2, 4, 3).reshape(b, dil, Lp, h)[:, :, :L]
    lse = lse.transpose(0, 2, 1, 3).reshape(b, s, h)
    return o, lse

def _swa_branch(qkv, positions, q_norm_w, k_norm_w):
    b, s, _ = qkv.shape
    q, k, v = jnp.split(qkv, 3, axis=-1)
    q = _rope(_rmsnorm(q.reshape(b, s, SWA_HEADS, HEAD_DIM), q_norm_w), positions)
    k = _rope(_rmsnorm(k.reshape(b, s, SWA_HEADS, HEAD_DIM), k_norm_w), positions)
    v = v.reshape(b, s, SWA_HEADS, HEAD_DIM)
    outs, lses = [], []
    for gi, (window, dil) in enumerate(SWA_GROUPS):
        hs = slice(gi * SWA_HEADS_PER_GROUP, (gi + 1) * SWA_HEADS_PER_GROUP)
        o, lse = _dilated_window_attention(q[:, :, hs], k[:, :, hs], v[:, :, hs], window // dil, dil)
        outs.append(o.astype(jnp.float32))
        lses.append(lse)
    wts = jax.nn.softmax(jnp.stack(lses), axis=0)
    o = jnp.sum(jnp.stack(outs) * wts[..., None], axis=0)
    return o.reshape(b, s, SWA_OUT_WIDTH).astype(qkv.dtype)

def setup_inputs(seed: int = 0) -> dict:
    key = jax.random.key(seed)
    ks = jax.random.split(key, 18)
    f32 = jnp.float32
    x = jax.random.normal(ks[0], (BATCH, SEQ, D_MODEL), f32)
    positions = jnp.broadcast_to(jnp.arange(SEQ, dtype=jnp.int32)[None, :], (BATCH, SEQ))
    ln1_w = 1.0 + 0.02 * jax.random.normal(ks[1], (DEPTH, D_MODEL), f32)
    w_in = jax.random.normal(ks[2], (DEPTH, D_MODEL, IN_COLS), f32) * D_MODEL ** -0.5
    gdn_conv_w = jax.random.normal(ks[3], (DEPTH, GDN_CONV, 3 * GDN_WIDTH), f32) * 0.5
    gdn_a_log = jnp.log(jax.random.uniform(ks[4], (DEPTH, GDN_HEADS), f32, 1.0, 16.0))
    dt = jnp.exp(jax.random.uniform(ks[5], (DEPTH, GDN_HEADS), f32, np.log(1e-3), np.log(1e-1)))
    gdn_dt_bias = dt + jnp.log(-jnp.expm1(-dt))
    gdn_norm_w = 1.0 + 0.02 * jax.random.normal(ks[6], (DEPTH, HEAD_DIM), f32)
    w_gdn_proj = jax.random.normal(ks[7], (DEPTH, GDN_WIDTH, D_MODEL), f32) * GDN_WIDTH ** -0.5
    swa_q_norm_w = 1.0 + 0.02 * jax.random.normal(ks[8], (DEPTH, HEAD_DIM), f32)
    swa_k_norm_w = 1.0 + 0.02 * jax.random.normal(ks[9], (DEPTH, HEAD_DIM), f32)
    w_swa_proj = jax.random.normal(ks[10], (DEPTH, SWA_OUT_WIDTH, D_MODEL), f32) * SWA_OUT_WIDTH ** -0.5
    w_out = jax.random.normal(ks[11], (DEPTH, D_MODEL, D_MODEL), f32) * D_MODEL ** -0.5
    ln2_w = 1.0 + 0.02 * jax.random.normal(ks[12], (DEPTH, D_MODEL), f32)
    w_ff1 = jax.random.normal(ks[13], (DEPTH, D_MODEL, D_FF), f32) * D_MODEL ** -0.5
    w_ff2 = jax.random.normal(ks[14], (DEPTH, D_FF, D_MODEL), f32) * D_FF ** -0.5
    return {"x": x, "positions": positions, "ln1_w": ln1_w, "w_in": w_in,
            "gdn_conv_w": gdn_conv_w, "gdn_a_log": gdn_a_log, "gdn_dt_bias": gdn_dt_bias,
            "gdn_norm_w": gdn_norm_w, "w_gdn_proj": w_gdn_proj,
            "swa_q_norm_w": swa_q_norm_w, "swa_k_norm_w": swa_k_norm_w,
            "w_swa_proj": w_swa_proj, "w_out": w_out, "ln2_w": ln2_w,
            "w_ff1": w_ff1, "w_ff2": w_ff2}

def reference(x, positions, ln1_w, w_in, gdn_conv_w, gdn_a_log, gdn_dt_bias, gdn_norm_w,
              w_gdn_proj, swa_q_norm_w, swa_k_norm_w, w_swa_proj, w_out, ln2_w, w_ff1, w_ff2):
    for l in range(DEPTH):
        h = _rmsnorm(x, ln1_w[l])
        proj = jnp.einsum("bsd,de->bse", h, w_in[l])
        gdn_qkv, gdn_z, gdn_a, gdn_b, swa_qkv, gate_a, gate_b = _split_cols(proj)
        o_a = _gdn_branch(gdn_qkv, gdn_z, gdn_a, gdn_b, gdn_conv_w[l], gdn_a_log[l],
                          gdn_dt_bias[l], gdn_norm_w[l])
        o_b = _swa_branch(swa_qkv, positions, swa_q_norm_w[l], swa_k_norm_w[l])
        y_a = jnp.einsum("bse,ed->bsd", o_a, w_gdn_proj[l])
        y_b = jnp.einsum("bse,ed->bsd", o_b, w_swa_proj[l])
        mixed = jax.nn.sigmoid(gate_a) * y_a + jax.nn.sigmoid(gate_b) * y_b
        x = x + jnp.einsum("bsd,de->bse", mixed, w_out[l])
        h = _rmsnorm(x, ln2_w[l])
        u = jax.nn.relu(jnp.einsum("bsd,df->bsf", h, w_ff1[l]))
        x = x + jnp.einsum("bsf,fd->bsd", jnp.square(u), w_ff2[l])
    return x


_drawn_inputs = setup_inputs


def setup_inputs(seed=0):
    import zlib

    import numpy as np

    out = dict(_drawn_inputs(seed))
    spreads = {}
    factors = {'ln1_w': 4.594,
     'gdn_norm_w': 8.0,
     'swa_q_norm_w': 8.0,
     'swa_k_norm_w': 8.0,
     'ln2_w': 13.141}
    for name, (base, spread) in spreads.items():
        noise = np.random.default_rng([zlib.crc32(name.encode()), seed]).standard_normal(out[name].shape)
        drawn = base * np.exp(spread * noise) if base else spread * noise
        out[name] = __import__('jax').numpy.asarray(drawn.astype(out[name].dtype))
    for name, factor in factors.items():
        out[name] = (out[name] * factor).astype(out[name].dtype)
    return out
```

```python
import math
from contextlib import ExitStack

import concourse.bass as bass
import numpy as np
from concourse import mybir

F32 = mybir.dt.float32
F32R = mybir.dt.float32r
I32 = mybir.dt.int32
ALU = mybir.AluOpType
ACT = mybir.ActivationFunctionType
AX_X = mybir.AxisListType.X

P = 128
TT = 2
D = 2048
KC = D // P
N = 512
EPS = 1e-6
HG = 8
GW = HG * P
CONV = 4
DILS = (1, 4, 16)
NG = len(DILS)
HS = 4
WINDOW = 128
SW = NG * HS * P
FF = 4 * D
SCALE = P ** -0.5
NEG = -1e30
SIG_MIN = -44.0
TWO_PI_PARTS = (6.28125, 0.0019350051879882812, 3.0199159819e-07)

COL_GDN = 0
COL_Z = 3 * GW
COL_AB = COL_Z + GW
COL_SWA = COL_AB + 2 * HG
COL_GA = COL_SWA + 3 * SW
COL_GB = COL_GA + D

BASE = 16512
RAW = 4
PIECES = 4
LEVELS = 6

EVENTS = """x_ready w_rows w_bcast w_head pos_ready w_ab ident_made ones_made tri_made res_made swa_mask_made
    gdn_mask_made pad_made rows_turned cols_made res_product res_mask x_turned x_split_hi x_split_lo
    x_square sincos table ab_hi ab_split a_sq a_ss a_ln a_rs a_t1 a_t2 a_t12 a_newton a_roped a_turned a_stored
    ab_done g_sums g_exps b_turned b_xc b_conv b_clamp b_sig b_silu b_sq b_ss b_nl b_rn b_out b_z w_q
    w_scores w_masked w_max w_nm w_exp w_pturned w_pt w_pv w_rs w_o n_load n_rg n_rb n_kv n_rows n_rk
    n_kd n_rv n_diff n_min n_decay n_kk n_lt0 n_LT n_aq0 n_aq n_Ls n_P n_Pc n_TU n_T n_U n_u n_w n_vn
    n_wT n_S n_o0 n_Sc n_ws n_qs n_vn1 n_qe n_o1 n_oc n_sq n_nss n_nl n_nr n_on n_out d_turned d_hi d_lo
    m_mixed x_back e_turned e_hi e_lo e_square u_squared u_turned u_hi u_lo stored c_gate angles ab_act
    ab_vec g_vec n_init""".split()


def build_block(nc, x, positions, inv_freq, ln1_w, w_in, conv_w, a_log, dt_bias, gdn_norm_w, w_gdn_proj,
                q_norm_w, k_norm_w, w_swa_proj, w_out, ln2_w, w_ff1, w_ff2, out):
    ctx = ExitStack()
    with ctx:
        KB = 1024

        def sb(name, shape, dt, at):
            return nc.alloc_sbuf_tensor_at(name, shape, dt, offset=int(at * KB) + BASE)

        raw = sb("raw", [P, RAW, 4, N], F32, 0)
        hi = sb("hi", [P, PIECES, 2, N], F32R, 32)
        lo = sb("lo", [P, PIECES, 2, N], F32R, 48)
        st_hi = sb("st_hi", [P, KC, TT * P], F32R, 64)
        st_lo = sb("st_lo", [P, KC, TT * P], F32R, 80)
        ident = sb("ident", [P, P], F32, 96)
        ones = sb("ones", [P, P], F32, 96.5)
        tri = sb("tri", [P, P], F32, 97)
        lncol = sb("lncol", [P, 2 * KC], F32, 97.5)
        convcol = sb("convcol", [P, CONV * 3 * HG], F32, 97.75)
        gnw = sb("gnw", [P, P], F32, 98.25)
        small = sb("small", [P, 256], F32, 98.75)
        ab_s = sb("ab_s", [P, TT, 2 * HG], F32, 99.75)
        gdn_qkv = sb("gdn_qkv", [P, 3, HG, TT * P], F32, 100)
        zs = sb("zs", [P, TT, HG, P], F32, 124)
        swa_mask = sb("swa_mask", [P, NG, 2, P], F32, 132)
        o_b = sb("o_b", [P, TT, HS * P], F32, 140)
        swa_qk = sb("swa_qk", [P, 2, NG * HS, TT * P], F32, 144)
        swa_v = sb("swa_v", [P, TT, SW], F32, 168)
        x_tok = sb("x_tok", [P, TT, D], F32, 100)
        x_scr = sb("x_scr", [P, D], F32, 116)
        rows = sb("rows", [P, 2, P], F32, 124)
        bc = sb("bc", [P, 2, P], F32, 125)
        ab_raw = sb("ab_raw", [P, KC, 2 * HG], F32, 126)
        ab_whi = sb("ab_whi", [P, KC, 2 * HG], F32R, 127)
        ab_wlo = sb("ab_wlo", [P, KC, 2 * HG], F32R, 128)
        pos_i = sb("pos_i", [P, TT], I32, 129)
        arg = sb("arg", [P, 2, TT, P // 2], F32, 129.25)
        turns = sb("turns", [P, 2, TT, P // 2], F32, 130.25)
        invf = sb("invf", [P, P // 2], F32, 131.25)
        res_ind = sb("res_ind", [16, NG, P], F32, 200.5)
        xs = sb("xs", [P, TT, HS, P], F32, 180)
        sq = sb("sq", [P, TT, HS, P], F32, 184)
        t1 = sb("t1", [P, TT, HS, P], F32, 188)
        t2 = sb("t2", [P, TT, HS, P], F32, 192)
        rope_c = sb("rope_c", [P, 2, TT, P], F32, 196)
        rope_s = sb("rope_s", [P, 2, TT, P], F32, 198)
        stage = sb("stage", [P, TT, N], F32, 180)
        xc = sb("xc", [P, HS, TT * P + CONV], F32, 184)
        y = sb("y", [P, HS, TT * P], F32, 188.25)
        e = sb("e", [P, HS, TT * P], F32, 192.25)
        qc = sb("qc", [P, NG, TT * P], F32, 196.25)
        sc = sb("sc", [P, NG * TT * P], F32, 199.25)
        pt = sb("pt", [P, NG * TT * P], F32, 202.25)
        gates = sb("gates", [P, 2, 4, TT, N], F32, 144)
        o_a = sb("o_a", [P, TT, HG, P], F32, 132)
        lmask = sb("lmask", [P, LEVELS + 1, P], F32, 203)
        kqv = sb("kqv", [P, 3, 4 * P], F32, 176)
        LT = sb("LT", [P, 4, P], F32, 182)
        aq = sb("aq", [P, 4, P], F32, 184)
        Ls = sb("Ls", [P, 2, 4, P], F32, 186)
        Pm = sb("Pm", [P, 4, P], F32, 190)
        Tm = sb("Tm", [P, 4, P], F32, 192)
        Um = sb("Um", [P, 4, P], F32, 194)
        rv = sb("rv", [P, 4, P], F32, 196)
        rk = sb("rk", [P, 4, P], F32, 198)
        kd = sb("kd", [P, 4, P], F32, 200)
        state = sb("state", [P, 2, P], F32, 202)
        mix_hi = sb("mix_hi", [P, KC, TT * P], F32R, 100)
        mix_lo = sb("mix_lo", [P, KC, TT * P], F32R, 116)
        mixed = sb("mixed", [P, TT, N], F32, 200)
        part_b = sb("part_b", [P, TT, N], F32, 132)
        o_hi = sb("o_hi", [P, HG + HS, TT * P], F32R, 176)
        o_lo = sb("o_lo", [P, HG + HS, TT * P], F32R, 188)
        x1 = sb("x1", [P, TT, D], F32, 144)
        x_scr2 = sb("x_scr2", [P, D], F32, 192)
        u_hi = sb("u_hi", [P, FF // 2 // P, TT * P], F32R, 100)
        u_lo = sb("u_lo", [P, FF // 2 // P, TT * P], F32R, 160)
        us = sb("us", [P, TT, N], F32, 192)
        uq = sb("uq", [P, TT, N], F32, 196)

        acc = ctx.enter_context(nc.psum_tensor("acc", [P, TT, N], F32))
        wk = ctx.enter_context(nc.psum_tensor("wk", [P, 6, N], F32))
        tb = wk[:, 0:2, :]
        tbv = tb.rearrange("p a (b t) -> p (a b) t", t=TT * P)

        def col(a, n):
            return small[:, a:a + n]
        ssx, lnx, rstd1 = col(0, 2), col(2, 2), col(4, 2)
        ss8, ln8, rs8 = col(8, 8), col(16, 8), col(24, 8)
        mx, nm, sm, rsm = col(32, 2), col(34, 2), col(36, 2), col(38, 2)
        posf = col(40, 2)
        alog_c, dt_c, ea_c = col(48, 8), col(56, 8), col(64, 8)
        beta, gg, Gc, kds, eG, beG, tmpa, tmpb, tmpc = (col(72 + 16 * n, 16) for n in range(9))
        nss, nln, nrs = col(216, 4), col(220, 4), col(224, 4)
        nt8 = col(234, 8)
        ssx2, lnx2, rstd2 = col(228, 2), col(230, 2), col(232, 2)

        def sem(name):
            return ctx.enter_context(nc.semaphore(name))

        landed = [sem(f"landed{i}") for i in range(RAW)]
        hi_ready, lo_ready = sem("hi_ready"), sem("lo_ready")
        piece_used = sem("piece_used")
        acc0_done = sem("acc0_done")
        acc_free = sem("acc_free")
        ev = {n: sem(n) for n in EVENTS}

        def wview(w):
            return w.rearrange("(k p) n -> p k n", p=P)
        w_in_v, w_a_v, w_b_v, w_o_v = wview(w_in), wview(w_gdn_proj), wview(w_swa_proj), wview(w_out)
        w_1_v, w_2_v = wview(w_ff1), wview(w_ff2)
        x_v = x.rearrange("(t p) d -> p t d", p=P)
        out_v = out.rearrange("(t p) d -> p t d", p=P)

        QA, QB, QC, QD = 0, 9, 17, 25
        QE = QD + 3
        QF0 = QE + 4
        QG0 = QF0 + 8
        QF1, QG1 = QG0 + 8, QG0 + 16
        Q_END = QG1 + 8
        GA_, GB_, GC_, GD_ = 0, 9, 17, 25
        GE = GD_ + 8
        GF0 = GE + 4
        GG0 = GF0 + 8
        GF1, GG1 = GG0 + 4, GG0 + 12

        def span(start, n):
            return slice(start, start + n) if isinstance(start, int) else bass.ds(start, n)

        def bcast(ap, axis, shape):
            return ap.unsqueeze(axis).to_broadcast(shape)

        block = ctx.enter_context(nc.Block())

        @block.sync
        def _(sp):
            def tile(q, j, w, k, c, first=False):
                if not first:
                    sp.wait_ge(lo_ready, 8 * q + 2 * j - 6)
                sp.dma_start(raw[:, j % RAW], w[:, k:k + 4, bass.ds(c, N)]).then_inc(landed[j % RAW], 16)

            def quad(q, w, k, c, first=False):
                for j in range(4):
                    tile(q, j, w, k + 4 * j, c, first)

            for t in range(TT):
                sp.dma_start(x_tok[:, t], x_v[:, t]).then_inc(ev["x_ready"], 16)
            quad(0, w_in_v, 0, COL_SWA, first=True)
            quad(1, w_in_v, 0, COL_SWA + SW)
            with sp.Fori(1, 3) as i:
                quad(2 * i, w_in_v, 0, COL_SWA + N * i)
                quad(2 * i + 1, w_in_v, 0, COL_SWA + SW + N * i)
            with sp.Fori(0, 3) as i:
                quad(QA + 6 + i, w_in_v, 0, COL_SWA + 2 * SW + N * i)
            with sp.Fori(0, 8) as i:
                quad(QB + i, w_in_v, 0, COL_GDN + N * i)
            with sp.Fori(0, 4) as i:
                quad(QC + 2 * i, w_in_v, 0, COL_GA + N * i)
                quad(QC + 2 * i + 1, w_in_v, 0, COL_GB + N * i)
            for cg in range(4):
                for j in range(3):
                    w, k = (w_a_v, 4 * j) if j < 2 else (w_b_v, 0)
                    tile(QD, 3 * cg + j, w, k, N * cg)
            quad(QE, w_o_v, 0, 0)
            sp.wait_ge(ev["m_mixed"], 4)
            sp.dma_start(x1[:], x_v).then_inc(ev["x_back"], 16)
            with sp.Fori(1, 4) as i:
                quad(QE + i, w_o_v, 0, N * i)
            for half, (qf, qg) in enumerate(((QF0, QG0), (QF1, QG1))):
                with sp.Fori(0, 8) as i:
                    quad(qf + i, w_1_v, 0, FF // 2 * half + N * i)
                with sp.Fori(0, 4) as i:
                    quad(qg + 2 * i, w_2_v, 32 * half, N * i)
                    quad(qg + 2 * i + 1, w_2_v, 32 * half + 16, N * i)

        @block.gpsimd
        def _(pool):
            def select(out_, pattern, base, cm, op, fill, after, done):
                pool.wait_ge(*after)
                pool.affine_select(out=out_, in_=out_, compare_op=op, fill=fill, base=base, pattern=pattern,
                                   channel_multiplier=cm).then_inc(done, 1)

            pool.memset(ident[:], 0.0).then_inc(ev["ident_made"], 1)
            pool.memset(ones[:], 1.0).then_inc(ev["ones_made"], 1)
            pool.memset(tri[:], 1.0).then_inc(ev["tri_made"], 1)
            pool.memset(res_ind[:], 0.0).then_inc(ev["res_made"], 1)
            select(ident[:], [[-1, P]], 0, 1, ALU.not_equal, 1.0, (ev["ident_made"], 1), ev["ident_made"])
            select(tri[:], [[1, P]], 0, -1, ALU.is_ge, 0.0, (ev["tri_made"], 1), ev["tri_made"])
            for g, dil in enumerate(DILS):
                v = res_ind[0:dil, g, :].rearrange("r (m q) -> r m q", q=dil)
                select(v, [[0, P // dil], [1, dil]], 0, -1, ALU.not_equal, 1.0, (ev["res_made"], 1 + g), ev["res_made"])
            pool.wait_ge(ev["res_mask"], 1)
            v = swa_mask[:, :, 1, :]
            select(v, [[0, NG], [-1, P]], 0, 1, ALU.is_ge, NEG, (ev["res_mask"], 1), ev["swa_mask_made"])
            for g, dil in enumerate(DILS):
                if WINDOW * dil < TT * P - 1:
                    select(swa_mask[:, g, 0, :], [[1, P]], WINDOW * dil - P, -1, ALU.is_ge, NEG,
                           (ev["swa_mask_made"], 1), ev["swa_mask_made"])
            pool.wait_ge(ev["w_pt"], 2 * HS)
            pool.wait_ge(ev["w_pv"], 2 * HS)
            pool.memset(lmask[:], 0.0).then_inc(ev["gdn_mask_made"], 1)
            made = 1
            for l in range(LEVELS + 1):
                h = 1 << l
                nb = P // (2 * h)
                v = lmask[:, l, :].rearrange("p (b two c) -> p b two c", two=2, c=h)[:, :, 1, :]
                pool.wait_ge(ev["gdn_mask_made"], made)
                pool.memset(v, 1.0).then_inc(ev["gdn_mask_made"], 1)
                select(v, [[-2 * h, nb], [0, h]], 0, 1, ALU.is_ge, 0.0, (ev["gdn_mask_made"], made + 1), ev["gdn_mask_made"])
                select(v, [[2 * h, nb], [0, h]], h - 1, -1, ALU.is_ge, 0.0, (ev["gdn_mask_made"], made + 2),
                       ev["gdn_mask_made"])
                made += 3
            pool.wait_ge(ev["gdn_mask_made"], made)
            with pool.Fori(0, 4) as i:
                pool.wait_ge(ev["n_LT"], i + 1)
                pool.wait_ge(ev["n_init"], 4 * i + 4)
                for l in range(LEVELS):
                    if l >= 2:
                        pool.wait_ge(ev["n_P"], 6 * i + l - 1)
                    pool.tensor_tensor(Ls[:, l % 2], LT[:], bcast(lmask[:, l + 1, :], 1, [P, 4, P]),
                                       ALU.mult).then_inc(ev["n_Ls"], 1)

        @block.tensor
        def _(pe):
            def group(q, g, n, sth, stl, i0=0, k0=0, mid={}, after={}):
                place = 0
                for pair in range(n // 2):
                    for t in range(TT):
                        for m in (2 * pair, 2 * pair + 1):
                            i = i0 + m
                            if t == 0:
                                pe.wait_ge(lo_ready, 8 * q + i + 1)
                            if m == 0:
                                pe.wait_ge(acc_free, 2 * g + 1 + t)
                            for kk in range(2):
                                for a, (w, v) in enumerate(((sth, hi), (stl, hi), (sth, lo))):
                                    last = pe.matmul(acc[:, t], w[:, k0 + 2 * m + kk, P * t:P * t + P],
                                                     v[:, i % PIECES, kk, :], start=m == 0 and kk == 0 and a == 0,
                                                     stop=m == n - 1 and kk == 1 and a == 2)
                            if t == 1:
                                last.then_inc(piece_used, 1)
                            elif m == n - 1:
                                last.then_inc(acc0_done, 1)
                            steps = after if place % 2 else mid
                            if place // 2 in steps:
                                steps[place // 2]()
                            place += 1

            def turn(src, dst, done):
                for b in range(4):
                    for t in range(TT):
                        last = pe.transpose(dst[:, b, P * t:P * t + P], src(t, b), ident[:])
                last.then_inc(done, 1)

            pe.wait_ge(ev["ident_made"], 2)
            pe.wait_ge(ev["w_rows"], 48)
            pe.transpose(wk[:, 4, 0:2 * KC], rows[0:2 * KC, 0, :], ident[0:2 * KC, 0:2 * KC])
            pe.transpose(wk[:, 4, P:P + 96], rows[0:96, 1, :], ident[0:96, 0:96]).then_inc(ev["rows_turned"], 1)
            pe.wait_ge(ev["res_made"], 1 + NG)
            for g, dil in enumerate(DILS):
                last = pe.matmul(wk[:, 5, P * g:P * g + P], res_ind[0:dil, g, :], res_ind[0:dil, g, :],
                                 start=True, stop=True)
            last.then_inc(ev["res_product"], 1)
            pe.wait_ge(ev["x_ready"], 32)
            for n, at in enumerate((0, 2, 4, 0)):
                if n == 2:
                    pe.wait_ge(ev["cols_made"], 2)
                    pe.wait_ge(ev["res_mask"], 1)
                if n == 3:
                    pe.wait_ge(ev["x_split_lo"], 4)
                dst = wk[:, at:at + 2, :].rearrange("p a (b t) -> p (a b) t", t=TT * P)
                turn(lambda t, b: x_tok[:, t, N * n + P * b:N * n + P * b + P], dst, ev["x_turned"])
            pe.sem_inc(piece_used, PIECES)
            pe.sem_inc(acc_free, TT)
            pe.wait_ge(ev["x_split_lo"], KC)

            def a_turn(n):
                def step():
                    pe.wait_ge(ev["a_roped"], n + 1)
                    if n:
                        pe.wait_ge(ev["a_stored"], n)
                    turn(lambda t, b: t1[:, t, b, :], tbv, ev["a_turned"])
                return step

            for g in range(9):
                group(g, g, 8, st_hi, st_lo, after={3: a_turn(g - 1)} if 1 <= g <= 6 else {})

            def b_turn(n):
                def step():
                    pe.wait_ge(acc_free, 2 * (GB_ + n) + 4)
                    if n:
                        pe.wait_ge(ev["b_out"], n)
                    else:
                        pe.wait_ge(ev["a_stored"], 6)
                    turn(lambda t, b: stage[:, t, P * b:P * b + P], tbv, ev["b_turned"])
                return step

            def b_ss(n):
                def step():
                    pe.wait_ge(ev["b_sq"], n + 1)
                    for a in range(2):
                        last = pe.matmul(tb[:, a, :], ones[:], e[:, 2 * a:2 * a + 2, :].rearrange("p b t -> p (b t)"),
                                         start=True, stop=True)
                    last.then_inc(ev["b_ss"], 1)
                return step

            def w_sc(h, t):
                n = 2 * h + t

                def step():
                    pe.wait_ge(ev["w_q"], h + 1)
                    if n:
                        pe.wait_ge(ev["w_pt"], n)
                    nk = (t + 1) * P
                    for g in range(NG):
                        last = pe.matmul(wk[:, 2 + g * nk // N, g * nk % N:g * nk % N + nk], qc[:, g, P * t:P * t + P],
                                         swa_qk[:, 1, HS * g + h, 0:nk], start=True, stop=True)
                    last.then_inc(ev["w_scores"], 1)
                return step

            def w_ptr(h, t):
                n = 2 * h + t

                def step():
                    pe.wait_ge(ev["w_exp"], n + 1)
                    for b in range(NG * (t + 1)):
                        last = pe.transpose(wk[:, 2 + b // 4, P * (b % 4):P * (b % 4) + P], sc[:, P * b:P * b + P],
                                            ident[:])
                    last.then_inc(ev["w_pturned"], 1)
                return step

            def w_pv(h, t):
                n = 2 * h + t

                def step():
                    pe.wait_ge(ev["w_pt"], n + 1)
                    if n:
                        pe.wait_ge(ev["w_o"], n)
                    for g in range(NG):
                        for kt in range(t + 1):
                            b = g * (t + 1) + kt
                            at = P * (HS * g + h)
                            last = pe.matmul(wk[:, 4, 0:P], pt[:, P * b:P * b + P], swa_v[:, kt, at:at + P],
                                             start=b == 0, stop=b == NG * (t + 1) - 1)
                    last.then_inc(ev["w_pv"], 1)
                return step

            pe.wait_ge(ev["ab_split"], 1)
            for t in range(TT):
                for k in range(KC):
                    for a, (w, v) in enumerate(((st_hi, ab_whi), (st_lo, ab_whi), (st_hi, ab_wlo))):
                        last = pe.matmul(wk[:, 5, 2 * HG * t:2 * HG * t + 2 * HG], w[:, k, P * t:P * t + P],
                                         v[:, k, :], start=k == 0 and a == 0, stop=k == KC - 1 and a == 2)
            last.then_inc(ev["ab_done"], 1)

            def g_sums():
                pe.wait_ge(ev["ab_vec"], 7)
                pe.matmul(wk[:, 5, 0:16], tri[:], gg, start=True, stop=True)
                pe.matmul(wk[:, 5, 16:32], ones[:], gg, start=True, stop=True).then_inc(ev["g_sums"], 1)

            for gi in range(8):
                h = gi // 2
                if gi % 2 == 0:
                    after = {0: w_sc(h, 0), 2: w_ptr(h, 0), 4: w_pv(h, 0), 6: w_sc(h, 1)}
                else:
                    after = {0: w_ptr(h, 1), 2: w_pv(h, 1)}
                if gi == 1:
                    after[7] = g_sums
                if 1 <= gi <= 6:
                    after[1] = b_turn(gi - 1)
                if 1 <= gi <= 4:
                    after[5] = b_ss(gi - 1)
                group(QB + gi, GB_ + gi, 8, st_hi, st_lo, after=after)

            W = [wk[:, 2 + n, :] for n in range(4)]

            def blk(ap, b):
                return ap[:, P * b:P * b + P]

            def gdn_steps(i):
                def turn_kv():
                    pe.wait_ge(ev["n_load"], i + 1)
                    pe.wait_ge(ev["n_rb"], i + 1)
                    for b in range(4):
                        pe.transpose(blk(W[0], b), blk(kqv[:, 1, :], b), ident[:])
                    for b in range(4):
                        last = pe.transpose(blk(W[1], b), blk(kqv[:, 2, :], b), ident[:])
                    last.then_inc(ev["n_kv"], 1)
                    pe.matmul(W[2], ones[:], Tm[:].rearrange("p b t -> p (b t)"), start=True, stop=True)
                    pe.matmul(W[3], ones[:], Um[:].rearrange("p b t -> p (b t)"), start=True, stop=True)\
                        .then_inc(ev["n_rows"], 1)

                def products():
                    pe.wait_ge(ev["n_rv"], i + 1)
                    for b in range(4):
                        pe.matmul(blk(W[0], b), blk(kqv[:, 1, :], b), blk(kqv[:, 1, :], b), start=True, stop=True)
                    for b in range(4):
                        last = pe.matmul(blk(W[1], b), blk(kqv[:, 1, :], b), blk(kqv[:, 0, :], b), start=True,
                                         stop=True)
                    last.then_inc(ev["n_kk"], 1)

                def level_a(l):
                    def step():
                        pe.wait_ge(ev["n_Ls"], 6 * i + l + 1)
                        if l:
                            pe.wait_ge(ev["n_T"], 5 * i + l)
                        else:
                            pe.wait_ge(ev["n_init"], 4 * i + 4)
                        for b in range(4):
                            last = pe.matmul(blk(W[0], b), Ls[:, l % 2, b, :], Tm[:, b, :], start=True, stop=True)
                        last.then_inc(ev["n_P"], 1)
                    return step

                def level_b(l):
                    h = 2 << l

                    def half(ap, which):
                        return ap.rearrange("p (n two c) -> p n two c", two=2, c=h)[:, :, which, :]

                    def step():
                        pe.wait_ge(ev["n_Pc"], 6 * i + l + 1)
                        if l:
                            pe.wait_ge(ev["n_U"], 6 * i + l)
                        if l < LEVELS - 1:
                            for b in range(4):
                                pe.matmul(W[1][:, 64 * b:64 * b + 64], Um[:, b, :], half(Pm[:, b, :], 0),
                                          start=True, stop=True)
                        for b in range(4):
                            last = pe.matmul(W[2][:, 64 * b:64 * b + 64], Pm[:, b, :], half(Um[:, b, :], 1),
                                             start=True, stop=True)
                        last.then_inc(ev["n_TU"], 1)
                    return step

                def solve():
                    pe.wait_ge(ev["n_U"], 6 * i + 6)
                    for b in range(4):
                        last = pe.matmul(blk(W[0], b), Um[:, b, :], rv[:, b, :], start=True, stop=True)
                    last.then_inc(ev["n_u"], 1)
                    for h in range(2):
                        last = pe.matmul(blk(W[1], h), rk[:, 2 * h + 1, :], Um[:, 2 * h + 1, :], start=True, stop=True)
                    last.then_inc(ev["n_w"], 1)

                def first_chunk():
                    pe.wait_ge(ev["n_vn"], i + 1)
                    for h in range(2):
                        last = pe.matmul(blk(W[2], h), kd[:, 2 * h, :], Pm[:, 2 * h, :], start=True, stop=True)
                    last.then_inc(ev["n_S"], 1)
                    for h in range(2):
                        last = pe.matmul(blk(W[3], 2 * h), aq[:, 2 * h, :], Pm[:, 2 * h, :], start=True, stop=True)
                    last.then_inc(ev["n_o0"], 1)

                def with_state():
                    pe.wait_ge(ev["n_wT"], i + 1)
                    pe.wait_ge(ev["n_Sc"], i + 1)
                    for h in range(2):
                        last = pe.matmul(blk(W[0], h), Tm[:, h, :], state[:, h, :], start=True, stop=True)
                    last.then_inc(ev["n_ws"], 1)
                    for h in range(2):
                        last = pe.matmul(blk(W[1], h), blk(kqv[:, 0, :], 2 * h + 1), state[:, h, :], start=True,
                                         stop=True)
                    last.then_inc(ev["n_qs"], 1)

                def second_chunk():
                    pe.wait_ge(ev["n_vn1"], i + 1)
                    for h in range(2):
                        last = pe.matmul(blk(W[3], 2 * h + 1), aq[:, 2 * h + 1, :], Pm[:, 2 * h + 1, :], start=True,
                                         stop=True)
                    last.then_inc(ev["n_o1"], 1)

                mid = {5 + l: level_a(l) for l in range(LEVELS)} | {11: solve, 12: first_chunk, 13: with_state,
                                                                    14: second_chunk}
                after = {5 + l: level_b(l) for l in range(LEVELS)} | {1: turn_kv, 3: products}
                return [({m - 8 * n: f for m, f in mid.items() if m // 8 == n},
                         {m - 8 * n: f for m, f in after.items() if m // 8 == n}) for n in range(2)]

            with pe.Fori(0, 4) as i:
                for n, (mid, after) in enumerate(gdn_steps(i)):
                    group(QC + n + 2 * i, GC_ + n + 2 * i, 8, st_hi, st_lo, mid=mid, after=after)

            pe.wait_ge(ev["n_out"], 4)
            for n, at in enumerate((0, 2, 4)):
                dst = wk[:, at:at + 2, :].rearrange("p a (b t) -> p (a b) t", t=TT * P)
                if n < 2:
                    turn(lambda t, b: o_a[:, t, 4 * n + b, :], dst, ev["d_turned"])
                else:
                    turn(lambda t, b: o_b[:, t, P * b:P * b + P], dst, ev["d_turned"])

            def m_turn(cg):
                def step():
                    pe.wait_ge(ev["m_mixed"], cg + 1)
                    pe.wait_ge(ev["d_lo"], 3 + cg)
                    turn(lambda t, b: mixed[:, t, P * b:P * b + P], tbv, ev["d_turned"])
                return step

            pe.wait_ge(ev["d_lo"], 3)
            for cg in range(4):
                group(QD, GD_ + 2 * cg, 4, o_hi, o_lo, i0=6 * cg, after={1: m_turn(cg - 1)} if cg else {})
                group(QD, GD_ + 2 * cg + 1, 2, o_hi, o_lo, i0=6 * cg + 4, k0=HG)

            def x_turn(g):
                def step():
                    pe.wait_ge(acc_free, 2 * g + 2 * GE + 4)
                    if g:
                        pe.wait_ge(ev["e_lo"], 4 * g)
                    else:
                        pe.wait_ge(ev["d_lo"], 7)
                    turn(lambda t, b: x1[:, t, N * g + P * b:N * g + P * b + P], tbv, ev["e_turned"])
                return step

            def last_mix():
                m_turn(3)()
            def after_last_mix():
                pe.wait_ge(ev["d_lo"], 7)
            group(QE, GE, 8, mix_hi, mix_lo, after={1: last_mix, 5: after_last_mix})
            for g in range(1, 4):
                group(QE + g, GE + g, 8, mix_hi, mix_lo, after={1: x_turn(g - 1)})

            def u_turn(half, g, first=False):
                def step():
                    pe.wait_ge(ev["u_squared"], g + 8 * half + 1)
                    if first:
                        if half == 0:
                            pe.wait_ge(ev["e_lo"], 16)
                        else:
                            pe.wait_ge(ev["u_lo"], 8)
                    else:
                        pe.wait_ge(ev["u_lo"], g + 8 * half)
                    turn(lambda t, b: uq[:, t, P * b:P * b + P], tbv, ev["u_turned"])
                return step

            def wait_e():
                pe.wait_ge(ev["e_lo"], 16)

            for half, (qf, qg, gf, gg_) in enumerate(((QF0, QG0, GF0, GG0), (QF1, QG1, GF1, GG1))):
                group(qf, gf, 8, st_hi, st_lo, after={} if half else {1: x_turn(3), 5: wait_e})
                group(qf + 1, gf + 1, 8, st_hi, st_lo, after={1: u_turn(half, 0, True)})
                with pe.Fori(0, 2) as r:
                    for g in (3 * r + 2, 3 * r + 3, 3 * r + 4):
                        group(qf + g, gf + g, 8, st_hi, st_lo, after={1: u_turn(half, g - 1)})

                def wait_u():
                    pe.wait_ge(ev["u_lo"], 8 * half + 8)
                group(qg, gg_, 16, u_hi, u_lo, after={1: u_turn(half, 7), 13: wait_u})
                for g in range(1, 4):
                    group(qg + 2 * g, gg_ + g, 16, u_hi, u_lo)

        @block.scalar
        def _(act):
            def split(q, i):
                act.wait_ge(landed[i // 2 % RAW], 16 * (q + i // 8) + 16)
                act.wait_ge(piece_used, 8 * q + i + 1)
                act.activation(hi[:, i % PIECES], raw[:, i // 2 % RAW, 2 * (i % 2):2 * (i % 2) + 2, :], ACT.Copy)\
                    .then_inc(hi_ready, 1)

            def ahead(q, n, steps={}, i0=0, last=False, read_out=()):
                for m in range(n):
                    if m in steps:
                        steps[m]()
                    if read_out and m >= n - 2:
                        read_out[m - (n - 2)]()
                    if not last or i0 + m + PIECES < n:
                        split(q, i0 + m + PIECES)

            def wait_apart(sem_, value):
                act.wait_ge(sem_, value)
                act.nop(nofuse=True)

            def f(out_, in_, func, wait, done, **kw):
                if wait is not None:
                    act.wait_ge(*wait)
                act.activation(out_, in_, func, **kw).then_inc(done, 1)

            def read_out(q, g, n, dst, func=ACT.Copy, scale=rstd1, before=None):
                def first():
                    if before is not None:
                        act.wait_ge(*before)
                    act.wait_ge(acc0_done, g + 1)
                    act.activation(dst(0), acc[:, 0], func, scale=scale[:, 0:1]).then_inc(acc_free, 1)

                def second():
                    act.wait_ge(piece_used, 8 * q + n + PIECES)
                    act.activation(dst(1), acc[:, 1], func, scale=scale[:, 1:2]).then_inc(acc_free, 1)
                return first, second

            act.preload_act_table_set("trig_and_small")
            act.dma_start(rows[0:KC, 0, :], ln1_w.rearrange("(k p) -> k p", p=P)).then_inc(ev["w_rows"], 16)
            act.dma_start(rows[KC:2 * KC, 0, :], ln2_w.rearrange("(k p) -> k p", p=P)).then_inc(ev["w_rows"], 16)
            act.dma_start(rows[0:96, 1, :], conv_w.rearrange("j (b p) -> (j b) p", p=P)).then_inc(ev["w_rows"], 16)
            with nc.allow_non_contiguous_dma(reason="256 positions"):
                act.dma_start(pos_i[:], positions.rearrange("(t p) -> p t", p=P)).then_inc(ev["pos_ready"], 16)
            act.dma_start(invf[:], inv_freq.partition_broadcast(P)).then_inc(ev["pos_ready"], 16)
            act.dma_start(bc[:, 0, :], q_norm_w.partition_broadcast(P)).then_inc(ev["w_bcast"], 16)
            act.dma_start(bc[:, 1, :], k_norm_w.partition_broadcast(P)).then_inc(ev["w_bcast"], 16)
            act.dma_start(gnw[:], gdn_norm_w.partition_broadcast(P)).then_inc(ev["w_head"], 16)
            act.dma_start(alog_c, a_log.partition_broadcast(P)).then_inc(ev["w_head"], 16)
            act.dma_start(dt_c, dt_bias.partition_broadcast(P)).then_inc(ev["w_head"], 16)
            act.dma_start(ab_raw[:], w_in_v[:, :, COL_AB:COL_AB + 2 * HG]).then_inc(ev["w_ab"], 16)
            act.wait_ge(ev["cols_made"], 1)
            for k in range(KC):
                act.wait_ge(ev["x_turned"], k // 4 + 1)
                src = wk[:, (0, 2, 4, 0)[k // 4] + k % 4 // 2, TT * P * (k % 2):TT * P * (k % 2) + TT * P]
                act.activation(st_hi[:, k], src, ACT.Copy, scale=lncol[:, k:k + 1]).then_inc(ev["x_split_hi"], 1)
            act.wait_ge(piece_used, PIECES)
            for i in range(PIECES):
                split(0, i)
            f(arg[:], arg[:], ACT.Sin, (ev["angles"], 13), ev["sincos"])
            act.preload_act_table_set("natural_log_exp_and_others")
            for t in range(TT):
                f(x_scr[:], x_tok[:, t], ACT.Square, (ev["x_square"], t) if t else None, ev["x_square"],
                  accum_out=ssx[:, t:t + 1])
            f(lnx, ssx, ACT.Ln, (ev["x_square"], 2), ev["x_square"], scale=1.0 / D, bias=EPS)
            f(rstd1, lnx, ACT.Exp, (ev["x_square"], 3), ev["x_square"], scale=-0.5)
            f(ab_whi[:], ab_raw[:], ACT.Copy, (ev["w_ab"], 16), ev["ab_hi"])
            act.wait_ge(ev["x_square"], 4)

            def a_store(which, i, n):
                def step():
                    act.wait_ge(ev["a_turned"], n + 1)
                    act.activation(swa_qk[:, which, HS * i:HS * i + HS, :], tbv, ACT.Copy)\
                        .then_inc(ev["a_stored"], 1)
                return step

            def a_group(q, n, steps={}):
                ahead(q, 8, steps, read_out=read_out(q, q, 8, lambda t: xs[:, t].rearrange("p h d -> p (h d)"),
                                                     before=(ev["a_t12"], n) if n else None))
                f(sq[:], xs[:], ACT.Square, (acc_free, 2 * q + 4), ev["a_sq"])
                f(ln8, ss8, ACT.Ln, (ev["a_ss"], n + 1), ev["a_ln"], scale=1.0 / P, bias=EPS)
                f(rs8, ln8, ACT.Exp, (ev["a_ln"], n + 1), ev["a_rs"], scale=-0.5)

            for n in range(6):
                a_group(QA + n, n, {4: a_store((n - 1) % 2, (n - 1) // 2, n - 1)} if n else {})
            for i in range(3):
                ahead(QA + 6 + i, 8, {} if i else {4: a_store(1, 2, 5)},
                      read_out=read_out(QA + 6 + i, GA_ + 6 + i, 8, lambda t, i=i: swa_v[:, t, N * i:N * i + N]))

            def w_load(h):
                if h:
                    act.wait_ge(ev["w_scores"], 2 * h)
                else:
                    act.wait_ge(ev["a_stored"], 6)
                act.activation(qc[:], swa_qk[:, 0, :, :].rearrange("p (g h) t -> p h g t", h=HS)[:, h], ACT.Copy)\
                    .then_inc(ev["w_q"], 1)

            def w_exp(h, t):
                n = 2 * h + t

                def step():
                    f(sc[:, 0:NG * (t + 1) * P], sc[:, 0:NG * (t + 1) * P], ACT.Exp, (ev["w_nm"], n + 1), ev["w_exp"],
                      scale=SCALE, bias=nm[:, t:t + 1], accum_out=sm[:, t:t + 1])
                return step

            def w_pt(h, t):
                n = 2 * h + t

                def step():
                    if n:
                        act.wait_ge(ev["w_pv"], n)
                    w = NG * (t + 1) * P
                    f(pt[:, 0:w], wk[:, 2:4, :].rearrange("p a n -> p (a n)")[:, 0:w], ACT.Copy,
                      (ev["w_pturned"], n + 1), ev["w_pt"])
                return step

            def both(*steps):
                def step():
                    for a in steps:
                        a()
                return step

            def b_xc(n):
                def step():
                    if n:
                        act.wait_ge(ev["b_conv"], 16 * n)
                    act.wait_ge(ev["pad_made"], 1)
                    f(xc[:, :, CONV - 1:CONV - 1 + TT * P], tbv, ACT.Copy, (ev["b_turned"], n + 1), ev["b_xc"])
                return step

            def b_sigmoid(n):
                def step():
                    f(e[:], e[:], ACT.Exp, (ev["b_clamp"], n + 1), ev["b_sig"], scale=-1.0)
                    f(e[:], e[:], ACT.Ln, (ev["b_sig"], 3 * n + 1), ev["b_sig"], bias=1.0)
                    f(e[:], e[:], ACT.Exp, (ev["b_sig"], 3 * n + 2), ev["b_sig"], scale=-1.0)
                return step

            def b_square(n):
                def step():
                    f(e[:], y[:], ACT.Square, (ev["b_silu"], n + 1), ev["b_sq"])
                return step

            def b_norm(n):
                def step():
                    f(e[:], tbv, ACT.Ln, (ev["b_ss"], n + 1), ev["b_nl"], bias=EPS)
                    f(e[:], e[:], ACT.Exp, (ev["b_nl"], n + 1), ev["b_rn"], scale=-0.5)
                return step

            def ab_chain():
                f(tmpa, tmpa, ACT.Exp, (ev["ab_vec"], 3), ev["ab_act"], scale=-1.0)
                f(tmpa, tmpa, ACT.Ln, (ev["ab_act"], 1), ev["ab_act"], bias=1.0)
                f(beta, tmpa, ACT.Exp, (ev["ab_act"], 2), ev["ab_act"], scale=-1.0)
                f(tmpc, tmpc, ACT.Exp, (ev["ab_vec"], 5), ev["ab_act"], scale=-1.0)
                f(tmpc, tmpc, ACT.Ln, (ev["ab_act"], 4), ev["ab_act"], bias=1.0)
                f(ea_c, alog_c, ACT.Exp, (ev["w_head"], 48), ev["ab_act"])

            def g_exps():
                f(eG, Gc, ACT.Exp, (ev["g_vec"], 1), ev["g_exps"])
                f(kds, kds, ACT.Exp, (ev["g_vec"], 2), ev["g_exps"])

            w_load(0)
            for gi in range(8):
                h = gi // 2
                n = gi - 1
                if gi % 2 == 0:
                    steps = {1: w_exp(h, 0), 3: w_pt(h, 0), 7: w_exp(h, 1)}
                else:
                    steps = {0: w_pt(h, 1)}
                if gi == 0:
                    steps[4] = ab_chain
                if gi == 2:
                    steps[0] = g_exps
                if 1 <= gi <= 6:
                    steps[1] = both(*(([steps[1]] if 1 in steps else []) + [b_xc(n)]))
                    steps[3] = both(*(([steps[3]] if 3 in steps else []) + [b_sigmoid(n)]))
                if 1 <= gi <= 4:
                    steps[4] = b_square(n)
                    steps[5] = b_norm(n)
                if gi == 7:
                    steps[4] = b_sigmoid(6)
                before = None if gi == 0 else (ev["b_turned"], gi) if gi < 7 else (ev["b_z"], 2)
                ahead(QB + gi, 8, steps, read_out=read_out(QB + gi, GB_ + gi, 8, lambda t: stage[:, t], before=before))
                if gi % 2 and gi < 7:
                    w_load(h + 1)
            b_sigmoid(7)()

            def gate(g, cnt, which, i):
                def step():
                    gt = gates[:, which, bass.ds(i, 1)].rearrange("p o t n -> p (o t) n")
                    wait_apart(acc_free, 2 * g + 4)
                    f(gt, gt, ACT.Exp, None, ev["c_gate"], scale=-1.0)
                    wait_apart(ev["c_gate"], 3 * cnt + 1)
                    f(gt, gt, ACT.Ln, None, ev["c_gate"], bias=1.0)
                    wait_apart(ev["c_gate"], 3 * cnt + 2)
                    f(gt, gt, ACT.Exp, None, ev["c_gate"], scale=-1.0)
                return step

            def gdn_steps(i):
                def load():
                    act.wait_ge(ev["b_out"], 6)
                    act.wait_ge(ev["b_z"], 4)
                    act.wait_ge(ev["w_pv"], 2 * HS)
                    f(kqv[:].rearrange("p w (h t) -> p w h t", h=2), gdn_qkv[:, :, bass.ds(2 * i, 2), :], ACT.Copy,
                      None, ev["n_load"])

                def decay():
                    f(Pm[:], Pm[:], ACT.Exp, (ev["n_min"], i + 1), ev["n_decay"])

                def copy_p(l):
                    def step():
                        f(Pm[:].rearrange("p b t -> p (b t)"), wk[:, 2, :], ACT.Copy, (ev["n_P"], 6 * i + l + 1), ev["n_Pc"])
                    return step

                def copy_w():
                    f(Tm[:, 0:2, :].rearrange("p b t -> p (b t)"), wk[:, 3, 0:2 * P], ACT.Copy, (ev["n_w"], i + 1), ev["n_wT"])

                def copy_s():
                    f(state[:].rearrange("p b t -> p (b t)"), wk[:, 4, 0:2 * P], ACT.Copy, (ev["n_S"], i + 1), ev["n_Sc"])

                def norm():
                    f(Ls[:, 0], LT[:], ACT.Square, (ev["n_oc"], 2 * i + 2), ev["n_sq"], scale=SCALE)
                    f(nln, nss, ACT.Ln, (ev["n_nss"], i + 1), ev["n_nl"], bias=P * EPS)
                    f(nrs, nln, ACT.Exp, (ev["n_nl"], i + 1), ev["n_nr"], scale=-0.5)

                steps = {0: load, 2: decay, 11: copy_w, 12: copy_s, 14: norm}
                steps |= {5 + l: copy_p(l) for l in range(LEVELS)}
                return steps

            with act.Fori(0, 4) as i:
                steps = gdn_steps(i)
                ahead(QC + 2 * i, 8, {m: a for m, a in steps.items() if m < 8})
                gate(GC_ + 2 * i, 2 * i, 0, i)()
                ahead(QC + 1 + 2 * i, 8, {m - 8: a for m, a in steps.items() if m >= 8})
                gate(GC_ + 1 + 2 * i, 2 * i + 1, 1, i)()

            for n in range(3):
                f(o_hi[:, 4 * n:4 * n + 4, :], wk[:, 2 * n:2 * n + 2, :].rearrange("p a (b t) -> p (a b) t", t=TT * P),
                  ACT.Copy, (ev["d_turned"], n + 1), ev["d_hi"])

            def m_hi(cg):
                def step():
                    f(mix_hi[:, 4 * cg:4 * cg + 4, :], tbv, ACT.Copy, (ev["d_turned"], 4 + cg), ev["d_hi"])
                return step

            for cg in range(4):
                ahead(QD, 4, {1: m_hi(cg - 1)} if cg else {}, i0=6 * cg)
                ahead(QD, 2, i0=6 * cg + 4)

            def x_hi(g):
                def step():
                    act.wait_ge(ev["e_turned"], g + 1)
                    for b in range(4):
                        act.activation(st_hi[:, 4 * g + b], tbv[:, b], ACT.Copy,
                                       scale=lncol[:, KC + 4 * g + b:KC + 4 * g + b + 1]).then_inc(ev["e_hi"], 1)
                return step

            ahead(QE, 8, {1: m_hi(3)})
            for g in range(1, 4):
                ahead(QE + g, 8, {1: x_hi(g - 1)})

            def x_stats():
                act.wait_ge(acc_free, 2 * (GE + 3) + 4)
                for t in range(TT):
                    f(x_scr2[:], x1[:, t], ACT.Square, (ev["e_square"], t) if t else None, ev["e_square"],
                      accum_out=ssx2[:, t:t + 1])
                f(lnx2, ssx2, ACT.Ln, (ev["e_square"], 2), ev["e_square"], scale=1.0 / D, bias=EPS)
                f(rstd2, lnx2, ACT.Exp, (ev["e_square"], 3), ev["e_square"], scale=-0.5)
                act.wait_ge(ev["e_square"], 4)

            def u_hi_step(half, g):
                def step():
                    wait_apart(ev["u_turned"], g + 8 * half + 1)
                    f(u_hi[:, span(4 * g, 4), :], tbv, ACT.Copy, None, ev["u_hi"])
                return step

            def u_group(q, g, n, steps):
                ahead(q, 8, steps, read_out=read_out(
                    q, g, 8, lambda t: us[:, t], func=ACT.Relu, scale=rstd2,
                    before=None if n is None else (ev["u_squared"], n)))

            for half, (qf, qg, gf, gg_) in enumerate(((QF0, QG0, GF0, GG0), (QF1, QG1, GF1, GG1))):
                if half:
                    u_group(qf, gf, 8, {})
                else:
                    u_group(qf, gf, None, {1: x_hi(3), 3: x_stats})
                u_group(qf + 1, gf + 1, 1 + 8 * half, {2: u_hi_step(half, 0)})
                with act.Fori(0, 2) as r:
                    for g in (3 * r + 2, 3 * r + 3, 3 * r + 4):
                        u_group(qf + g, gf + g, g + 8 * half, {2: u_hi_step(half, g - 1)})
                ahead(qg, 16, {2: u_hi_step(half, 7)})
                if half == 0:
                    for g in range(1, 4):
                        ahead(qg + 2 * g, 16)
                else:
                    def store(g):
                        act.wait_ge(acc_free, 2 * g + 2 * gg_ + 4)
                        act.dma_start(out_v[:, :, N * g:N * g + N], x1[:, :, N * g:N * g + N])\
                            .then_inc(ev["stored"], 16)
                    for g in range(1, 3):
                        ahead(qg + 2 * g, 16, {2: lambda: store(g - 1)})
                    ahead(qg + 6, 16, {2: lambda: store(2)}, last=True)
                    store(3)
                    act.wait_ge(ev["stored"], 64)

        @block.vector
        def _(dve):
            def split(q, i):
                dve.wait_ge(hi_ready, 8 * q + i + 1)
                dve.tensor_tensor(lo[:, i % PIECES], raw[:, i // 2 % RAW, 2 * (i % 2):2 * (i % 2) + 2, :],
                                  hi[:, i % PIECES].bitcast(F32), ALU.subtract).then_inc(lo_ready, 1)

            def ahead(q, n, steps={}, i0=0, last=False, read_out=()):
                for m in range(n):
                    if m in steps:
                        steps[m]()
                    if read_out and m >= n - 2:
                        read_out[m - (n - 2)]()
                    if not last or i0 + m + PIECES < n:
                        split(q, i0 + m + PIECES)

            def tt_(out_, a, b, op, wait, done):
                if wait is not None:
                    dve.wait_ge(*wait)
                dve.tensor_tensor(out_, a, b, op).then_inc(done, 1)

            def ts_(out_, a, s1, s2, op0, op1, wait, done):
                if wait is not None:
                    dve.wait_ge(*wait)
                if s2 is None:
                    dve.tensor_scalar(out_, a, s1, None, op0).then_inc(done, 1)
                else:
                    dve.tensor_scalar(out_, a, s1, s2, op0, op1).then_inc(done, 1)

            dve.wait_ge(ev["rows_turned"], 1)
            dve.tensor_copy(lncol[:], wk[:, 4, 0:2 * KC]).then_inc(ev["cols_made"], 1)
            dve.tensor_copy(convcol[:], wk[:, 4, P:P + 96]).then_inc(ev["cols_made"], 1)
            dve.wait_ge(ev["res_product"], 1)
            for a in range(2):
                last = dve.tensor_scalar(swa_mask[:, :, a, :], wk[:, 5, 0:NG * P].rearrange("p (g k) -> p g k", g=NG),
                                         1.0, -NEG, ALU.subtract, ALU.mult)
            last.then_inc(ev["res_mask"], 1)
            for k in range(KC):
                dve.wait_ge(ev["x_split_hi"], k // 2 * 2 + 2)
                src = wk[:, (0, 2, 4, 0)[k // 4] + k % 4 // 2, TT * P * (k % 2):TT * P * (k % 2) + TT * P]
                dve.scalar_tensor_tensor(out=st_lo[:, k], in0=src, scalar=lncol[:, k:k + 1],
                                         in1=st_hi[:, k].bitcast(F32), op0=ALU.mult, op1=ALU.subtract)\
                    .then_inc(ev["x_split_lo"], 1)
            dve.wait_ge(ev["pos_ready"], 32)
            dve.tensor_copy(posf, pos_i[:]).then_inc(ev["angles"], 1)
            for t in range(TT):
                ts_(arg[:, 0, t, :], invf[:], posf[:, t:t + 1], None, ALU.mult, None, (ev["angles"], 1), ev["angles"])
            for i in range(PIECES):
                split(0, i)
            dve.wait_ge(ev["angles"], 3)
            dve.tensor_copy(arg[:, 1], arg[:, 0]).then_inc(ev["angles"], 1)
            magic = 1.5 * 2.0 ** 23
            for a in range(2):
                ts_(turns[:, a], arg[:, a], 1.0 / (2 * math.pi), 0.25 * a, ALU.mult, ALU.add, (ev["angles"], 4), ev["angles"])
            ts_(turns[:], turns[:], magic, None, ALU.add, None, (ev["angles"], 6), ev["angles"])
            ts_(turns[:], turns[:], magic, None, ALU.subtract, None, (ev["angles"], 7), ev["angles"])
            for n, part in enumerate(TWO_PI_PARTS):
                dve.wait_ge(ev["angles"], 8 + n)
                dve.scalar_tensor_tensor(out=arg[:], in0=turns[:], scalar=-part, in1=arg[:], op0=ALU.mult,
                                         op1=ALU.add).then_inc(ev["angles"], 1)
            ts_(arg[:, 1], arg[:, 1], math.pi / 2, None, ALU.add, None, (ev["angles"], 11), ev["angles"])
            pi_in = 3.1415925
            ts_(arg[:], arg[:], pi_in, -pi_in, ALU.min, ALU.max, (ev["angles"], 12), ev["angles"])
            dve.wait_ge(ev["sincos"], 1)
            dve.wait_ge(ev["w_bcast"], 32)
            for w in range(2):
                for half in range(2):
                    a = slice(64 * half, 64 * half + 64)
                    other = slice(64 - 64 * half, 128 - 64 * half)
                    dve.tensor_tensor(rope_c[:, w, :, a], arg[:, 1], bcast(bc[:, w, a], 1, [P, TT, 64]), ALU.mult)\
                        .then_inc(ev["table"], 1)
                    dve.scalar_tensor_tensor(out=rope_s[:, w, :, a], in0=arg[:, 0], scalar=-1.0 if half == 0 else 1.0,
                                             in1=bcast(bc[:, w, other], 1, [P, TT, 64]), op0=ALU.mult, op1=ALU.mult)\
                        .then_inc(ev["table"], 1)
            dve.wait_ge(ev["ab_hi"], 1)
            dve.tensor_tensor(ab_wlo[:], ab_raw[:], ab_whi[:].bitcast(F32), ALU.subtract).then_inc(ev["ab_split"], 1)
            dve.wait_ge(ev["table"], 8)

            def a_post(w, n):
                dve.wait_ge(ev["a_sq"], n + 1)
                dve.tensor_reduce(ss8, sq[:].rearrange("p t h d -> p (t h) d"), AX_X, ALU.add).then_inc(ev["a_ss"], 1)
                if n:
                    dve.wait_ge(ev["a_turned"], n)
                tt_(t1[:], xs[:], bcast(rope_c[:, w], 2, [P, TT, HS, P]), ALU.mult, None, ev["a_t1"])
                tt_(t2[:, :, :, 0:64], xs[:, :, :, 64:128], bcast(rope_s[:, w, :, 0:64], 2, [P, TT, HS, 64]),
                    ALU.mult, None, ev["a_t2"])
                tt_(t2[:, :, :, 64:128], xs[:, :, :, 0:64], bcast(rope_s[:, w, :, 64:128], 2, [P, TT, HS, 64]),
                    ALU.mult, None, ev["a_t2"])
                dve.wait_ge(ev["a_t2"], 2 * n + 2)
                tt_(t1[:], t1[:], t2[:], ALU.add, (ev["a_t1"], n + 1), ev["a_t12"])
                dve.wait_ge(ev["a_t12"], n + 1)
                t1f = t1[:].rearrange("p t h d -> p (t h) d")
                dve.wait_ge(ev["a_rs"], n + 1)
                ts_(ln8, ss8, 1.0 / P, EPS, ALU.mult, ALU.add, None, ev["a_newton"])
                tt_(nt8, rs8, rs8, ALU.mult, None, ev["a_newton"])
                tt_(nt8, nt8, ln8, ALU.mult, (ev["a_newton"], 5 * n + 2), ev["a_newton"])
                ts_(nt8, nt8, -0.5, 1.5, ALU.mult, ALU.add, (ev["a_newton"], 5 * n + 3), ev["a_newton"])
                tt_(rs8, rs8, nt8, ALU.mult, (ev["a_newton"], 5 * n + 4), ev["a_newton"])
                tt_(t1f, t1f, bcast(rs8, 2, [P, TT * HS, P]), ALU.mult, (ev["a_newton"], 5 * n + 5), ev["a_roped"])

            for n in range(6):
                ahead(QA + n, 8)
                a_post(n % 2, n)
            for i in range(3):
                ahead(QA + 6 + i, 8)

            dve.wait_ge(ev["a_turned"], 6)
            dve.memset(xc[:, :, 0:CONV - 1], 0.0).then_inc(ev["pad_made"], 1)

            def w_soft(h, t):
                n = 2 * h + t
                w = NG * (t + 1) * P

                def step():
                    if n:
                        dve.wait_ge(ev["w_pturned"], n)
                    dve.wait_ge(ev["swa_mask_made"], 2)
                    mask = swa_mask[:] if t else swa_mask[:, :, 1:2, :]
                    v = "p (g a k) -> p g a k"
                    tt_(sc[:, 0:w].rearrange(v, g=NG, a=t + 1),
                        wk[:, 2:4, :].rearrange("p a n -> p (a n)")[:, 0:w].rearrange(v, g=NG, a=t + 1), mask,
                        ALU.add, (ev["w_scores"], n + 1), ev["w_masked"])
                    dve.wait_ge(ev["w_masked"], n + 1)
                    dve.tensor_reduce(mx[:, t:t + 1], sc[:, 0:w], AX_X, ALU.max).then_inc(ev["w_max"], 1)
                    ts_(nm[:, t:t + 1], mx[:, t:t + 1], -SCALE, None, ALU.mult, None, (ev["w_max"], n + 1), ev["w_nm"])
                return step

            def w_out_(h, t):
                n = 2 * h + t

                def step():
                    dve.wait_ge(ev["w_exp"], n + 1)
                    dve.reciprocal(rsm[:, t:t + 1], sm[:, t:t + 1]).then_inc(ev["w_rs"], 1)
                    dve.wait_ge(ev["w_rs"], n + 1)
                    ts_(o_b[:, t, P * h:P * h + P], wk[:, 4, 0:P], rsm[:, t:t + 1], None, ALU.mult, None,
                        (ev["w_pv"], n + 1), ev["w_o"])
                return step

            def b_conv(n):
                def step():
                    dve.wait_ge(ev["b_xc"], n + 1)
                    if n:
                        dve.wait_ge(ev["b_out"], n)
                    for j in range(CONV):
                        for b in range(4):
                            c = 3 * HG * j + 4 * n + b
                            src = xc[:, b, j:j + TT * P]
                            if j == 0:
                                dve.tensor_scalar(y[:, b], src, convcol[:, c:c + 1], None, ALU.mult)\
                                    .then_inc(ev["b_conv"], 1)
                            else:
                                dve.wait_ge(ev["b_conv"], 16 * n + 4 * j + b - 3)
                                dve.scalar_tensor_tensor(out=y[:, b], in0=src, scalar=convcol[:, c:c + 1], in1=y[:, b],
                                                         op0=ALU.mult, op1=ALU.add).then_inc(ev["b_conv"], 1)
                    ts_(e[:], y[:], SIG_MIN, None, ALU.max, None, (ev["b_conv"], 16 * n + 16), ev["b_clamp"])
                return step

            def b_silu(n):
                def step():
                    if n < 4:
                        tt_(y[:], y[:], e[:], ALU.mult, (ev["b_sig"], 3 * n + 3), ev["b_silu"])
                    else:
                        tt_(gdn_qkv[:, 2, 4 * (n - 4):4 * (n - 4) + 4, :], y[:], e[:], ALU.mult, (ev["b_sig"], 3 * n + 3),
                            ev["b_out"])
                return step

            def b_scaled(n):
                def step():
                    tt_(gdn_qkv[:, n // 2, 4 * (n % 2):4 * (n % 2) + 4, :], y[:], e[:], ALU.mult, (ev["b_rn"], n + 1),
                        ev["b_out"])
                return step

            def z_clamp(n):
                def step():
                    dve.wait_ge(acc_free, 2 * (GB_ + n) + 4)
                    ts_(e[:].rearrange("p b t -> p (b t)"), stage[:].rearrange("p a n -> p (a n)"), SIG_MIN, None,
                        ALU.max, None, (ev["b_out"], 6), ev["b_clamp"])
                return step

            def z_out(n):
                a = n - 6

                def step():
                    v = zs[:, :, 4 * a:4 * a + 4, :].rearrange("p t h d -> p t (h d)")
                    sig = e[:].rearrange("p b t -> p (b t)").rearrange("p (a n) -> p a n", a=TT)
                    tt_(v, stage[:], sig, ALU.mult, (ev["b_sig"], 3 * n + 3), ev["b_z"])
                    w = zs[:, :, 4 * a:4 * a + 4, :]
                    dve.wait_ge(ev["b_z"], 2 * a + 1)
                    tt_(w, w, gnw[:].unsqueeze(1).unsqueeze(1).to_broadcast([P, TT, 4, P]), ALU.mult,
                        (ev["w_head"], 48), ev["b_z"])
                return step

            def by_head(ap):
                return ap.rearrange("p (h t) -> p t h", t=TT)

            def ab_chain():
                dve.wait_ge(ev["ab_done"], 1)
                dve.wait_ge(ev["w_head"], 48)
                for t in range(TT):
                    ts_(ab_s[:, t], wk[:, 5, 16 * t:16 * t + 16], rstd1[:, t:t + 1], None, ALU.mult, None, None,
                        ev["ab_vec"])
                ts_(by_head(tmpa), ab_s[:, :, HG:2 * HG], SIG_MIN, None, ALU.max, None, (ev["ab_vec"], 2), ev["ab_vec"])
                tt_(by_head(tmpb), ab_s[:, :, 0:HG], bcast(dt_c, 1, [P, TT, HG]), ALU.add, None, ev["ab_vec"])
                dve.wait_ge(ev["ab_vec"], 4)
                dve.scalar_tensor_tensor(out=tmpc, in0=tmpb, scalar=-1.0, in1=tmpb, op0=ALU.mult, op1=ALU.max)\
                    .then_inc(ev["ab_vec"], 1)
                dve.wait_ge(ev["ab_act"], 5)
                dve.scalar_tensor_tensor(out=tmpc, in0=tmpb, scalar=0.0, in1=tmpc, op0=ALU.max, op1=ALU.add)\
                    .then_inc(ev["ab_vec"], 1)
                dve.wait_ge(ev["ab_act"], 6)
                dve.wait_ge(ev["ab_vec"], 6)
                dve.scalar_tensor_tensor(out=by_head(gg), in0=by_head(tmpc), scalar=-1.0,
                                         in1=bcast(ea_c, 1, [P, TT, HG]), op0=ALU.mult, op1=ALU.mult)\
                    .then_inc(ev["ab_vec"], 1)

            def g_consts():
                dve.wait_ge(ev["g_sums"], 1)
                dve.tensor_copy(Gc, wk[:, 5, 0:16]).then_inc(ev["g_vec"], 1)
                tt_(kds, wk[:, 5, 16:32], Gc, ALU.subtract, (ev["g_vec"], 1), ev["g_vec"])
                tt_(beG, beta, eG, ALU.mult, (ev["g_exps"], 1), ev["g_vec"])

            def both(*steps):
                def step():
                    for a in steps:
                        a()
                return step

            for gi in range(8):
                h = gi // 2
                n = gi - 1
                if gi % 2 == 0:
                    steps = {0: w_soft(h, 0), 5: w_out_(h, 0), 6: w_soft(h, 1)}
                else:
                    steps = {3: w_out_(h, 1)}
                if gi == 0:
                    steps[4] = ab_chain
                if gi == 2:
                    steps[0] = both(g_consts, steps[0])
                if 1 <= gi <= 6:
                    steps[1] = b_conv(n)
                    steps[4] = b_silu(n)
                if 1 <= gi <= 4:
                    steps[6] = both(b_scaled(n), *([steps[6]] if 6 in steps else []))
                if gi == 7:
                    steps[2] = z_clamp(6)
                    steps[5] = z_out(6)
                ahead(QB + gi, 8, steps)
            z_clamp(7)()
            z_out(7)()
            dve.wait_ge(ev["b_z"], 4)

            def gate(q, g, which, i):
                gt = gates[:, which, bass.ds(i, 1)].rearrange("p o t n -> p (o t) n")

                def first():
                    dve.wait_ge(acc0_done, g + 1)
                    dve.tensor_scalar(gt[:, 0], acc[:, 0], rstd1[:, 0:1], SIG_MIN, ALU.mult, ALU.max)\
                        .then_inc(acc_free, 1)

                def second():
                    dve.wait_ge(piece_used, 8 * q + 8 + PIECES)
                    dve.tensor_scalar(gt[:, 1], acc[:, 1], rstd1[:, 1:2], SIG_MIN, ALU.mult, ALU.max)\
                        .then_inc(acc_free, 1)
                return first, second

            def flat(ap):
                return ap.rearrange("p b t -> p (b t)")

            def gdn_steps(i):
                def cols(ap):
                    return bcast(ap[:, bass.ds(4 * i, 4)], 2, [P, 4, P])

                def rows_in():
                    dve.wait_ge(ev["w_pv"], 2 * HS)
                    tt_(Tm[:], bcast(tri[:], 1, [P, 4, P]), cols(gg), ALU.mult, (ev["g_vec"], 3), ev["n_rg"])
                    tt_(Um[:], bcast(ident[:], 1, [P, 4, P]), cols(beta), ALU.mult, None, ev["n_rb"])

                def w(n):
                    return wk[:, 2 + n, :].rearrange("p (b t) -> p b t", t=P)

                def factors():
                    tt_(rk[:], w(0), cols(beG), ALU.mult, (ev["n_kv"], i + 1), ev["n_rk"])
                    tt_(kd[:], w(0), cols(kds), ALU.mult, (ev["g_exps"], 2), ev["n_kd"])
                    tt_(rv[:], w(1), cols(beta), ALU.mult, None, ev["n_rv"])
                    tt_(Pm[:], w(2), cols(Gc), ALU.subtract, (ev["n_rows"], i + 1), ev["n_diff"])
                    ts_(Pm[:], Pm[:], 0.0, None, ALU.min, None, (ev["n_diff"], i + 1), ev["n_min"])

                def system():
                    dve.wait_ge(ev["n_decay"], i + 1)
                    tt_(LT[:], w(0), Pm[:], ALU.mult, (ev["n_kk"], i + 1), ev["n_lt0"])
                    tt_(aq[:], w(1), Pm[:], ALU.mult, None, ev["n_aq0"])
                    tt_(LT[:], w(3), LT[:], ALU.mult, (ev["n_lt0"], i + 1), ev["n_LT"])
                    tt_(aq[:], aq[:], bcast(tri[:], 1, [P, 4, P]), ALU.mult, (ev["n_aq0"], i + 1), ev["n_aq"])
                    dve.wait_ge(ev["gdn_mask_made"], 1 + 3 * (LEVELS + 1))
                    tt_(Um[:], LT[:], bcast(lmask[:, 0, :], 1, [P, 4, P]), ALU.mult, (ev["n_LT"], i + 1), ev["n_init"])
                    dve.wait_ge(ev["n_init"], 4 * i + 1)
                    dve.transpose(flat(Tm[:]), flat(Um[:])).then_inc(ev["n_init"], 1)
                    tt_(Tm[:], bcast(ident[:], 1, [P, 4, P]), Tm[:], ALU.subtract, (ev["n_init"], 4 * i + 2), ev["n_init"])
                    tt_(Um[:], bcast(ident[:], 1, [P, 4, P]), Um[:], ALU.subtract, None, ev["n_init"])

                def level(l):
                    h = 2 << l

                    def half(ap, which):
                        return flat(ap).rearrange("p (n two c) -> p n two c", two=2, c=h)[:, :, which, :]

                    def step():
                        dve.wait_ge(ev["n_TU"], 6 * i + l + 1)
                        if l < LEVELS - 1:
                            v = half(Tm[:], 0)
                            tt_(v, v, wk[:, 3, 0:256].rearrange("p (n c) -> p n c", c=h), ALU.subtract,
                                (ev["n_T"], 5 * i + l) if l else (ev["n_init"], 4 * i + 4), ev["n_T"])
                        v = half(Um[:], 1)
                        tt_(v, v, wk[:, 4, 0:256].rearrange("p (n c) -> p n c", c=h), ALU.subtract,
                            (ev["n_U"], 6 * i + l) if l else (ev["n_init"], 4 * i + 4), ev["n_U"])
                    return step

                def copy_u():
                    dve.wait_ge(ev["n_u"], i + 1)
                    dve.tensor_copy(flat(Pm[:]), wk[:, 2, :]).then_inc(ev["n_vn"], 1)

                def second(ap):
                    return ap.rearrange("p (h c) d -> p h c d", c=2)[:, :, 1, :]

                def first_(ap):
                    return ap.rearrange("p (h c) d -> p h c d", c=2)[:, :, 0, :]

                def less_state():
                    dve.wait_ge(ev["n_vn"], i + 1)
                    v = second(Pm[:])
                    tt_(v, v, wk[:, 2, 0:2 * P].rearrange("p (h d) -> p h d", h=2), ALU.subtract, (ev["n_ws"], i + 1),
                        ev["n_vn1"])
                    g2 = eG[:, bass.ds(4 * i, 4)].rearrange("p (h c) -> p h c", c=2)[:, :, 1:2].to_broadcast([P, 2, P])
                    tt_(rk[:, 0:2, :], wk[:, 3, 0:2 * P].rearrange("p (h d) -> p h d", h=2), g2, ALU.mult,
                        (ev["n_qs"], i + 1), ev["n_qe"])

                def output():
                    dve.wait_ge(ev["n_o1"], i + 1)
                    dve.tensor_copy(first_(LT[:]), first_(w(3))).then_inc(ev["n_oc"], 1)
                    tt_(second(LT[:]), second(w(3)), rk[:, 0:2, :], ALU.add, (ev["n_qe"], i + 1), ev["n_oc"])
                    dve.wait_ge(ev["n_sq"], i + 1)
                    dve.tensor_reduce(nss, Ls[:, 0], AX_X, ALU.add).then_inc(ev["n_nss"], 1)
                    tt_(LT[:], LT[:], bcast(nrs, 2, [P, 4, P]), ALU.mult, (ev["n_nr"], i + 1), ev["n_on"])

                    def heads(ap):
                        return ap[:, :, bass.ds(2 * i, 2), :].rearrange("p t h d -> p h t d")
                    dve.wait_ge(ev["n_on"], i + 1)
                    tt_(heads(o_a), LT[:].rearrange("p (h c) d -> p h c d", c=2), heads(zs), ALU.mult, None, ev["n_out"])

                steps = {0: rows_in, 1: factors, 3: system, 11: copy_u, 13: less_state, 14: output}
                steps |= {5 + l: level(l) for l in range(LEVELS)}
                return steps

            with dve.Fori(0, 4) as i:
                steps = gdn_steps(i)
                ahead(QC + 2 * i, 8, {m: a for m, a in steps.items() if m < 8},
                      read_out=gate(QC + 2 * i, GC_ + 2 * i, 0, i))
                ahead(QC + 1 + 2 * i, 8, {m - 8: a for m, a in steps.items() if m >= 8},
                      read_out=gate(QC + 1 + 2 * i, GC_ + 1 + 2 * i, 1, i))

            for n in range(3):
                tt_(o_lo[:, 4 * n:4 * n + 4, :], wk[:, 2 * n:2 * n + 2, :].rearrange("p a (b t) -> p (a b) t", t=TT * P),
                    o_hi[:, 4 * n:4 * n + 4, :].bitcast(F32), ALU.subtract, (ev["d_hi"], n + 1), ev["d_lo"])

            def m_lo(cg):
                def step():
                    tt_(mix_lo[:, 4 * cg:4 * cg + 4, :], tbv, mix_hi[:, 4 * cg:4 * cg + 4, :].bitcast(F32),
                        ALU.subtract, (ev["d_hi"], 4 + cg), ev["d_lo"])
                return step

            dve.wait_ge(ev["c_gate"], 24)

            def gated(cg, branch, dst, pieces):
                def first():
                    if branch == 0 and cg:
                        dve.wait_ge(ev["d_turned"], 3 + cg)
                    dve.wait_ge(acc0_done, GD_ + 2 * cg + branch + 1)
                    dve.tensor_tensor(dst[:, 0], acc[:, 0], gates[:, branch, cg, 0, :], ALU.mult).then_inc(acc_free, 1)

                def second():
                    dve.wait_ge(piece_used, 8 * QD + pieces + PIECES)
                    dve.tensor_tensor(dst[:, 1], acc[:, 1], gates[:, branch, cg, 1, :], ALU.mult).then_inc(acc_free, 1)
                return first, second

            for cg in range(4):
                ahead(QD, 4, {1: m_lo(cg - 1)} if cg else {}, i0=6 * cg, read_out=gated(cg, 0, mixed, 6 * cg + 4))
                ahead(QD, 2, i0=6 * cg + 4, read_out=gated(cg, 1, part_b, 6 * cg + 6))
                dve.wait_ge(acc_free, 2 * (GD_ + 2 * cg + 1) + 4)
                dve.tensor_tensor(mixed[:], mixed[:], part_b[:], ALU.add).then_inc(ev["m_mixed"], 1)

            def x_lo(g):
                def step():
                    for b in range(4):
                        k = 4 * g + b
                        dve.wait_ge(ev["e_hi"], 4 * g + b // 2 * 2 + 2)
                        dve.scalar_tensor_tensor(out=st_lo[:, k], in0=tbv[:, b], scalar=lncol[:, KC + k:KC + k + 1],
                                                 in1=st_hi[:, k].bitcast(F32), op0=ALU.mult, op1=ALU.subtract)\
                            .then_inc(ev["e_lo"], 1)
                return step

            def add(q, g, n, cols):
                def first():
                    dve.wait_ge(acc0_done, g + 1)
                    dve.tensor_tensor(x1[:, 0, cols], acc[:, 0], x1[:, 0, cols], ALU.add).then_inc(acc_free, 1)

                def second():
                    dve.wait_ge(piece_used, 8 * q + n + PIECES)
                    dve.tensor_tensor(x1[:, 1, cols], acc[:, 1], x1[:, 1, cols], ALU.add).then_inc(acc_free, 1)
                return first, second

            dve.wait_ge(ev["x_back"], 16)
            for g in range(4):
                ahead(QE + g, 8, {1: x_lo(g - 1) if g else m_lo(3)}, read_out=add(QE + g, GE + g, 8, span(N * g, N)))

            def u_lo_step(half, g):
                def step():
                    a = span(4 * g, 4)
                    tt_(u_lo[:, a, :], tbv, u_hi[:, a, :].bitcast(F32), ALU.subtract, (ev["u_hi"], g + 8 * half + 1),
                        ev["u_lo"])
                return step

            def u_square(g, n, first=False):
                dve.wait_ge(acc_free, 2 * g + 4)
                if not first:
                    dve.wait_ge(ev["u_turned"], n)
                dve.tensor_tensor(uq[:], us[:], us[:], ALU.mult).then_inc(ev["u_squared"], 1)

            for half, (qf, qg, gf, gg_) in enumerate(((QF0, QG0, GF0, GG0), (QF1, QG1, GF1, GG1))):
                ahead(qf, 8, {} if half else {1: x_lo(3)})
                u_square(gf, 8 * half, first=half == 0)
                ahead(qf + 1, 8, {2: u_lo_step(half, 0)})
                u_square(gf + 1, 1 + 8 * half)
                with dve.Fori(0, 2) as r:
                    for g in (3 * r + 2, 3 * r + 3, 3 * r + 4):
                        ahead(qf + g, 8, {2: u_lo_step(half, g - 1)})
                        u_square(gf + g, g + 8 * half)
                for g in range(4):
                    ahead(qg + 2 * g, 16, {} if g else {2: u_lo_step(half, 7)}, last=half == 1 and g == 3,
                          read_out=add(qg + 2 * g, gg_ + g, 16, span(N * g, N)))


def kernel(**inputs):
    import concourse.bacc as bacc
    from concourse.bass_utils import run_bass_kernel_spmd

    nc = bacc.Bacc("TRN2", target_bir_lowering=False, num_devices=1)
    half = P // 2
    arrays = {
        "x": inputs["x"][0], "positions": inputs["positions"][0],
        "inv_freq": np.power(np.float32(10000.0), -np.arange(half, dtype=np.float32) / np.float32(half)),
        "ln1_w": inputs["ln1_w"][0], "w_in": inputs["w_in"][0], "conv_w": inputs["gdn_conv_w"][0],
        "a_log": inputs["gdn_a_log"][0], "dt_bias": inputs["gdn_dt_bias"][0], "gdn_norm_w": inputs["gdn_norm_w"][0],
        "w_gdn_proj": inputs["w_gdn_proj"][0], "q_norm_w": inputs["swa_q_norm_w"][0],
        "k_norm_w": inputs["swa_k_norm_w"][0], "w_swa_proj": inputs["w_swa_proj"][0], "w_out": inputs["w_out"][0],
        "ln2_w": inputs["ln2_w"][0], "w_ff1": inputs["w_ff1"][0], "w_ff2": inputs["w_ff2"][0],
    }
    arrays = {f"in_{n}": np.ascontiguousarray(a) for n, a in arrays.items()}
    args = [nc.dram_tensor(n, a.shape, mybir.dt.from_np(a.dtype), kind="ExternalInput").ap()
            for n, a in arrays.items()]
    out = nc.dram_tensor("out_x", (TT * P, D), F32, kind="ExternalOutput").ap()
    build_block(nc, *args, out)
    r = run_bass_kernel_spmd(nc, [arrays], core_ids=[0])
    return r.results[0]["out_x"].reshape(1, TT * P, D)
```

```python
import math
from contextlib import ExitStack

import concourse.bass as bass
import numpy as np
from concourse import mybir

F32 = mybir.dt.float32
F32R = mybir.dt.float32r
I32 = mybir.dt.int32
ALU = mybir.AluOpType
ACT = mybir.ActivationFunctionType
AX_X = mybir.AxisListType.X

P = 128
TT = 2
D = 2048
KC = D // P
N = 512
EPS = 1e-6
HG = 8
GW = HG * P
CONV = 4
DILS = (1, 4, 16)
NG = len(DILS)
HS = 4
WINDOW = 128
SW = NG * HS * P
FF = 4 * D
SCALE = P ** -0.5
NEG = -1e30
SIG_MIN = -44.0
TWO_PI_PARTS = (6.28125, 0.0019350051879882812, 3.0199159819e-07)

COL_GDN = 0
COL_Z = 3 * GW
COL_AB = COL_Z + GW
COL_SWA = COL_AB + 2 * HG
COL_GA = COL_SWA + 3 * SW
COL_GB = COL_GA + D

BASE = 1152
RAW = 4
PIECES = 4
FIRST_SPLITS = {3: (0, 1), 7: (2,), 11: (3,)}
LEVELS = 6

EVENTS = """x_left x_right w_rows w_bcast w_head pos_ready w_ab ident_made ones_made tri_made res_made swa_mask_made
    gdn_mask_made pad_made rows_turned cols_made res_product res_mask x_turned x_split_hi x_split_lo
    x_square sincos table ab_hi ab_split a_sq a_ss a_ln a_rs a_t1 a_t2 a_t12 a_newton a_roped a_turned a_stored
    ab_done g_sums g_exps b_turned b_xc b_conv b_clamp b_sig b_silu b_sq b_ss b_nl b_rn b_out b_z w_q
    w_scores w_masked w_max w_nm w_exp w_pturned w_pt w_pv w_rs w_o n_load n_rg n_rb n_kv n_rows n_rk
    n_kd n_rv n_diff n_min n_decay n_kk n_lt0 n_LT n_aq0 n_aq n_Ls n_P n_Pc n_TU n_T n_U n_u n_w n_vn
    n_wT n_S n_o0 n_Sc n_ws n_qs n_vn1 n_qe n_o1 n_oc n_sq n_nss n_nl n_nr n_on n_out d_turned d_hi d_lo
    m_mixed x_back e_turned e_hi e_lo e_square u_squared u_turned u_hi u_lo stored c_gate angles ab_act
    ab_vec g_vec n_init""".split()


def build_block(nc, x, positions, inv_freq, ln1_w, w_in, conv_w, a_log, dt_bias, gdn_norm_w, w_gdn_proj,
                q_norm_w, k_norm_w, w_swa_proj, w_out, ln2_w, w_ff1, w_ff2, out):
    ctx = ExitStack()
    with ctx:
        KB = 1024

        def sb(name, shape, dt, at):
            return nc.alloc_sbuf_tensor_at(name, shape, dt, offset=int(at * KB) + BASE)

        raw = sb("raw", [P, RAW, 4, N], F32, 0)
        hi = sb("hi", [P, PIECES, 2, N], F32R, 32)
        lo = sb("lo", [P, PIECES, 2, N], F32R, 48)
        st_hi = sb("st_hi", [P, KC, TT * P], F32R, 64)
        st_lo = sb("st_lo", [P, KC, TT * P], F32R, 80)
        ident = sb("ident", [P, P], F32, 96)
        ones = sb("ones", [P, P], F32, 96.5)
        tri = sb("tri", [P, P], F32, 97)
        lncol = sb("lncol", [P, 2 * KC], F32, 97.5)
        convcol = sb("convcol", [P, CONV * 3 * HG], F32, 97.75)
        gnw = sb("gnw", [P, P], F32, 98.25)
        small = sb("small", [P, 256], F32, 98.75)
        ab_s = sb("ab_s", [P, TT, 2 * HG], F32, 99.75)
        gdn_qkv = sb("gdn_qkv", [P, 3, HG, TT * P], F32, 100)
        zs = sb("zs", [P, TT, HG, P], F32, 124)
        swa_mask = sb("swa_mask", [P, NG, 2, P], F32, 132)
        o_b = sb("o_b", [P, TT, HS * P], F32, 140)
        swa_qk = sb("swa_qk", [P, 2, NG * HS, TT * P], F32, 144)
        swa_v = sb("swa_v", [P, TT, SW], F32, 168)
        x_tok = sb("x_tok", [P, TT, D], F32, 100)
        x_scr = sb("x_scr", [P, D], F32, 116)
        rows = sb("rows", [P, 2, P], F32, 124)
        bc = sb("bc", [P, 2, P], F32, 125)
        ab_raw = sb("ab_raw", [P, KC, 2 * HG], F32, 126)
        ab_whi = sb("ab_whi", [P, KC, 2 * HG], F32R, 127)
        ab_wlo = sb("ab_wlo", [P, KC, 2 * HG], F32R, 128)
        pos_i = sb("pos_i", [P, TT], I32, 129)
        arg = sb("arg", [P, 2, TT, P // 2], F32, 129.25)
        turns = sb("turns", [P, 2, TT, P // 2], F32, 130.25)
        invf = sb("invf", [P, P // 2], F32, 131.25)
        res_ind = sb("res_ind", [16, NG, P], F32, 200.5)
        xs = sb("xs", [P, TT, HS, P], F32, 180)
        sq = sb("sq", [P, TT, HS, P], F32, 184)
        t1 = sb("t1", [P, TT, HS, P], F32, 188)
        t2 = sb("t2", [P, TT, HS, P], F32, 192)
        rope_c = sb("rope_c", [P, 2, TT, P], F32, 196)
        rope_s = sb("rope_s", [P, 2, TT, P], F32, 198)
        stage = sb("stage", [P, TT, N], F32, 180)
        xc = sb("xc", [P, HS, TT * P + CONV], F32, 184)
        y2 = [sb("y_even", [P, HS, TT * P], F32, 188.25), sb("y_odd", [P, HS, TT * P], F32, 206.5)]
        e2 = [sb("e_even", [P, HS, TT * P], F32, 192.25), sb("e_odd", [P, HS, TT * P], F32, 210.5)]
        qc = sb("qc", [P, NG, TT * P], F32, 196.25)
        sc = sb("sc", [P, NG * TT * P], F32, 199.25)
        pt = sb("pt", [P, NG * TT * P], F32, 202.25)
        gates = sb("gates", [P, 2, 4, TT, N], F32, 144)
        o_a = sb("o_a", [P, TT, HG, P], F32, 132)
        lmask = sb("lmask", [P, LEVELS + 1, P], F32, 203)
        kqv = sb("kqv", [P, 3, 4 * P], F32, 176)
        LT = sb("LT", [P, 4, P], F32, 182)
        aq = sb("aq", [P, 4, P], F32, 184)
        Ls = sb("Ls", [P, 2, 4, P], F32, 186)
        Pm = sb("Pm", [P, 4, P], F32, 190)
        Tm = sb("Tm", [P, 4, P], F32, 192)
        Um = sb("Um", [P, 4, P], F32, 194)
        rv = sb("rv", [P, 4, P], F32, 196)
        rk = sb("rk", [P, 4, P], F32, 198)
        kd = sb("kd", [P, 4, P], F32, 200)
        state = sb("state", [P, 2, P], F32, 202)
        mix_hi = sb("mix_hi", [P, KC, TT * P], F32R, 100)
        mix_lo = sb("mix_lo", [P, KC, TT * P], F32R, 116)
        mixed = sb("mixed", [P, TT, N], F32, 140)
        part_b = sb("part_b", [P, 4, TT, N], F32, 198)
        oa_hi = sb("oa_hi", [P, HG, TT * P], F32R, 176)
        oa_lo = sb("oa_lo", [P, HG, TT * P], F32R, 184)
        ob_hi = sb("ob_hi", [P, HS, TT * P], F32R, 214.75)
        ob_lo = sb("ob_lo", [P, HS, TT * P], F32R, 218.75)
        x1 = sb("x1", [P, TT, D], F32, 144)
        x_scr2 = sb("x_scr2", [P, D], F32, 192)
        u_hi = sb("u_hi", [P, FF // 2 // P, TT * P], F32R, 100)
        u_lo = sb("u_lo", [P, FF // 2 // P, TT * P], F32R, 160)
        us = sb("us", [P, TT, N], F32, 192)
        uq = sb("uq", [P, TT, N], F32, 196)

        acc = ctx.enter_context(nc.psum_tensor("acc", [P, TT, N], F32))
        wk = ctx.enter_context(nc.psum_tensor("wk", [P, 6, N], F32))
        tb = wk[:, 0:2, :]
        tbv = tb.rearrange("p a (b t) -> p (a b) t", t=TT * P)

        def col(a, n):
            return small[:, a:a + n]
        ssx, lnx, rstd1 = col(0, 2), col(2, 2), col(4, 2)
        ss8, ln8, rs8 = col(8, 8), col(16, 8), col(24, 8)
        mx, nm, sm, rsm = col(32, 2), col(34, 2), col(36, 2), col(38, 2)
        posf = col(40, 2)
        alog_c, dt_c, ea_c = col(48, 8), col(56, 8), col(64, 8)
        beta, gg, Gc, kds, eG, beG, tmpa, tmpb, tmpc = (col(72 + 16 * n, 16) for n in range(9))
        nss, nln, nrs = col(216, 4), col(220, 4), col(224, 4)
        nt8 = col(234, 8)
        ssx2, lnx2, rstd2 = col(228, 2), col(230, 2), col(232, 2)

        def sem(name):
            return ctx.enter_context(nc.semaphore(name))

        landed = [sem(f"landed{i}") for i in range(RAW)]
        hi_ready, lo_ready = sem("hi_ready"), sem("lo_ready")
        piece_used = sem("piece_used")
        acc0_done = sem("acc0_done")
        acc_free = sem("acc_free")
        ev = {n: sem(n) for n in EVENTS}

        def wview(w):
            return w.rearrange("(k p) n -> p k n", p=P)
        w_in_v, w_a_v, w_b_v, w_o_v = wview(w_in), wview(w_gdn_proj), wview(w_swa_proj), wview(w_out)
        w_1_v, w_2_v = wview(w_ff1), wview(w_ff2)
        x_v = x.rearrange("(t p) d -> p t d", p=P)
        out_v = out.rearrange("(t p) d -> p t d", p=P)

        QA, QB, QC, QD = 0, 9, 17, 25
        QE = QD + 3
        QF0 = QE + 4
        QG0 = QF0 + 8
        QF1, QG1 = QG0 + 8, QG0 + 16
        Q_END = QG1 + 8
        GA_, GB_, GC_, GD_ = 0, 9, 17, 25
        GE = GD_ + 8
        GF0 = GE + 4
        GG0 = GF0 + 8
        GF1, GG1 = GG0 + 4, GG0 + 12

        def span(start, n):
            return slice(start, start + n) if isinstance(start, int) else bass.ds(start, n)

        def bcast(ap, axis, shape):
            return ap.unsqueeze(axis).to_broadcast(shape)

        block = ctx.enter_context(nc.Block())

        @block.sync
        def _(sp):
            def tile(q, j, w, k, c, first=False):
                if not first:
                    sp.wait_ge(lo_ready, 8 * q + 2 * j - 6)
                sp.dma_start(raw[:, j % RAW], w[:, k:k + 4, bass.ds(c, N)]).then_inc(landed[j % RAW], 16)

            def quad(q, w, k, c, first=False):
                for j in range(4):
                    tile(q, j, w, k + 4 * j, c, first)

            sp.dma_start(rows[0:KC, 0, :], ln1_w.rearrange("(k p) -> k p", p=P)).then_inc(ev["w_rows"], 16)
            sp.dma_start(rows[KC:2 * KC, 0, :], ln2_w.rearrange("(k p) -> k p", p=P)).then_inc(ev["w_rows"], 16)
            sp.dma_start(rows[0:96, 1, :], conv_w.rearrange("j (b p) -> (j b) p", p=P)).then_inc(ev["w_rows"], 16)
            sp.dma_start(x_tok[:, :, 0:D // 2], x_v[:, :, 0:D // 2]).then_inc(ev["x_left"], 16)
            sp.dma_start(x_tok[:, :, D // 2:D], x_v[:, :, D // 2:D]).then_inc(ev["x_right"], 16)
            quad(0, w_in_v, 0, COL_SWA, first=True)
            quad(1, w_in_v, 0, COL_SWA + SW)
            with sp.Fori(1, 3) as i:
                quad(2 * i, w_in_v, 0, COL_SWA + N * i)
                quad(2 * i + 1, w_in_v, 0, COL_SWA + SW + N * i)
            with sp.Fori(0, 3) as i:
                quad(QA + 6 + i, w_in_v, 0, COL_SWA + 2 * SW + N * i)
            with sp.Fori(0, 8) as i:
                quad(QB + i, w_in_v, 0, COL_GDN + N * i)
            with sp.Fori(0, 4) as i:
                quad(QC + 2 * i, w_in_v, 0, COL_GA + N * i)
                quad(QC + 2 * i + 1, w_in_v, 0, COL_GB + N * i)
            for cg in range(4):
                tile(QD, cg, w_b_v, 0, N * cg)
            for cg in range(4):
                for j in range(2):
                    tile(QD, 4 + 2 * cg + j, w_a_v, 4 * j, N * cg)
            quad(QE, w_o_v, 0, 0)
            sp.wait_ge(ev["m_mixed"], 4)
            sp.dma_start(x1[:], x_v).then_inc(ev["x_back"], 16)
            with sp.Fori(1, 4) as i:
                quad(QE + i, w_o_v, 0, N * i)
            for half, (qf, qg) in enumerate(((QF0, QG0), (QF1, QG1))):
                with sp.Fori(0, 8) as i:
                    quad(qf + i, w_1_v, 0, FF // 2 * half + N * i)
                with sp.Fori(0, 4) as i:
                    quad(qg + 2 * i, w_2_v, 32 * half, N * i)
                    quad(qg + 2 * i + 1, w_2_v, 32 * half + 16, N * i)

        @block.gpsimd
        def _(pool):
            def select(out_, pattern, base, cm, op, fill, after, done):
                pool.wait_ge(*after)
                pool.affine_select(out=out_, in_=out_, compare_op=op, fill=fill, base=base, pattern=pattern,
                                   channel_multiplier=cm).then_inc(done, 1)

            pool.memset(ident[:], 0.0).then_inc(ev["ident_made"], 1)
            pool.memset(ones[:], 1.0).then_inc(ev["ones_made"], 1)
            pool.memset(tri[:], 1.0).then_inc(ev["tri_made"], 1)
            pool.memset(res_ind[:], 0.0).then_inc(ev["res_made"], 1)
            select(ident[:], [[-1, P]], 0, 1, ALU.not_equal, 1.0, (ev["ident_made"], 1), ev["ident_made"])
            select(tri[:], [[1, P]], 0, -1, ALU.is_ge, 0.0, (ev["tri_made"], 1), ev["tri_made"])
            for g, dil in enumerate(DILS):
                v = res_ind[0:dil, g, :].rearrange("r (m q) -> r m q", q=dil)
                select(v, [[0, P // dil], [1, dil]], 0, -1, ALU.not_equal, 1.0, (ev["res_made"], 1 + g), ev["res_made"])
            pool.wait_ge(ev["res_mask"], 1)
            v = swa_mask[:, :, 1, :]
            select(v, [[0, NG], [-1, P]], 0, 1, ALU.is_ge, NEG, (ev["res_mask"], 1), ev["swa_mask_made"])
            for g, dil in enumerate(DILS):
                if WINDOW * dil < TT * P - 1:
                    select(swa_mask[:, g, 0, :], [[1, P]], WINDOW * dil - P, -1, ALU.is_ge, NEG,
                           (ev["swa_mask_made"], 1), ev["swa_mask_made"])
            pool.wait_ge(ev["w_pt"], 2 * HS)
            pool.wait_ge(ev["w_pv"], 2 * HS)
            pool.memset(lmask[:], 0.0).then_inc(ev["gdn_mask_made"], 1)
            made = 1
            for l in range(LEVELS + 1):
                h = 1 << l
                nb = P // (2 * h)
                v = lmask[:, l, :].rearrange("p (b two c) -> p b two c", two=2, c=h)[:, :, 1, :]
                pool.wait_ge(ev["gdn_mask_made"], made)
                pool.memset(v, 1.0).then_inc(ev["gdn_mask_made"], 1)
                select(v, [[-2 * h, nb], [0, h]], 0, 1, ALU.is_ge, 0.0, (ev["gdn_mask_made"], made + 1),
                       ev["gdn_mask_made"])
                select(v, [[2 * h, nb], [0, h]], h - 1, -1, ALU.is_ge, 0.0, (ev["gdn_mask_made"], made + 2),
                       ev["gdn_mask_made"])
                made += 3
            pool.wait_ge(ev["gdn_mask_made"], made)
            with pool.Fori(0, 4) as i:
                pool.wait_ge(ev["n_LT"], i + 1)
                pool.wait_ge(ev["n_init"], 4 * i + 4)
                for l in range(LEVELS):
                    if l >= 2:
                        pool.wait_ge(ev["n_P"], 6 * i + l - 1)
                    pool.tensor_tensor(Ls[:, l % 2], LT[:], bcast(lmask[:, l + 1, :], 1, [P, 4, P]),
                                       ALU.mult).then_inc(ev["n_Ls"], 1)

        @block.tensor
        def _(pe):
            def group(q, g, n, sth, stl, i0=0, k0=0, mid={}, after={}):
                place = 0
                for pair in range(n // 2):
                    for t in range(TT):
                        for m in (2 * pair, 2 * pair + 1):
                            i = i0 + m
                            if t == 0:
                                pe.wait_ge(lo_ready, 8 * q + i + 1)
                            if m == 0:
                                pe.wait_ge(acc_free, 2 * g + 1 + t)
                            for kk in range(2):
                                for a, (w, v) in enumerate(((sth, hi), (stl, hi), (sth, lo))):
                                    last = pe.matmul(acc[:, t], w[:, k0 + 2 * m + kk, P * t:P * t + P],
                                                     v[:, i % PIECES, kk, :], start=m == 0 and kk == 0 and a == 0,
                                                     stop=m == n - 1 and kk == 1 and a == 2)
                            if t == 1:
                                last.then_inc(piece_used, 1)
                            elif m == n - 1:
                                last.then_inc(acc0_done, 1)
                            steps = after if place % 2 else mid
                            if place // 2 in steps:
                                steps[place // 2]()
                            place += 1

            def turn(src, dst, done):
                for b in range(4):
                    for t in range(TT):
                        last = pe.transpose(dst[:, b, P * t:P * t + P], src(t, b), ident[:])
                last.then_inc(done, 1)

            pe.wait_ge(ev["ident_made"], 2)
            pe.wait_ge(ev["w_rows"], 48)
            pe.transpose(wk[:, 4, 0:2 * KC], rows[0:2 * KC, 0, :], ident[0:2 * KC, 0:2 * KC])
            pe.transpose(wk[:, 4, P:P + 96], rows[0:96, 1, :], ident[0:96, 0:96]).then_inc(ev["rows_turned"], 1)
            pe.wait_ge(ev["res_made"], 1 + NG)
            for g, dil in enumerate(DILS):
                last = pe.matmul(wk[:, 5, P * g:P * g + P], res_ind[0:dil, g, :], res_ind[0:dil, g, :],
                                 start=True, stop=True)
            last.then_inc(ev["res_product"], 1)
            for n, at in enumerate((0, 2, 4, 0)):
                pe.wait_ge(ev["x_left" if n < 2 else "x_right"], 16)
                if n == 2:
                    pe.wait_ge(ev["cols_made"], 2)
                    pe.wait_ge(ev["res_mask"], 1)
                if n == 3:
                    pe.wait_ge(ev["x_split_lo"], 4)
                dst = wk[:, at:at + 2, :].rearrange("p a (b t) -> p (a b) t", t=TT * P)
                turn(lambda t, b: x_tok[:, t, N * n + P * b:N * n + P * b + P], dst, ev["x_turned"])
            pe.sem_inc(piece_used, PIECES)
            pe.sem_inc(acc_free, TT)
            pe.wait_ge(ev["x_split_lo"], 4)

            def x_chunks(n):
                return lambda: pe.wait_ge(ev["x_split_lo"], n)

            def a_turn(n):
                def step():
                    pe.wait_ge(ev["a_roped"], n + 1)
                    if n:
                        pe.wait_ge(ev["a_stored"], n)
                    turn(lambda t, b: t1[:, t, b, :], tbv, ev["a_turned"])
                return step

            for g in range(9):
                if g == 0:
                    after = {1: x_chunks(8), 3: x_chunks(12), 5: x_chunks(16)}
                else:
                    after = {3: a_turn(g - 1)} if g <= 6 else {}
                group(g, g, 8, st_hi, st_lo, after=after)

            def b_turn(n):
                def step():
                    pe.wait_ge(acc_free, 2 * (GB_ + n) + 4)
                    if n == 0:
                        pe.wait_ge(ev["a_stored"], 6)
                    elif n == 1:
                        pe.wait_ge(ev["b_xc"], 1)
                    elif n <= 5:
                        pe.wait_ge(ev["b_nl"], n - 1)
                    turn(lambda t, b: stage[:, t, P * b:P * b + P], tbv, ev["b_turned"])
                return step

            def b_ss(n):
                def step():
                    pe.wait_ge(ev["b_xc"], n + 2)
                    pe.wait_ge(ev["b_sq"], n + 1)
                    for a in range(2):
                        squares = e2[n % 2][:, 2 * a:2 * a + 2, :].rearrange("p b t -> p (b t)")
                        last = pe.matmul(tb[:, a, :], ones[:], squares, start=True, stop=True)
                    last.then_inc(ev["b_ss"], 1)
                return step

            def w_sc(h, t):
                n = 2 * h + t

                def step():
                    pe.wait_ge(ev["w_q"], h + 1)
                    if n:
                        pe.wait_ge(ev["w_pt"], n)
                    nk = (t + 1) * P
                    for g in range(NG):
                        last = pe.matmul(wk[:, 2 + g * nk // N, g * nk % N:g * nk % N + nk], qc[:, g, P * t:P * t + P],
                                         swa_qk[:, 1, HS * g + h, 0:nk], start=True, stop=True)
                    last.then_inc(ev["w_scores"], 1)
                return step

            def w_ptr(h, t):
                n = 2 * h + t

                def step():
                    pe.wait_ge(ev["w_exp"], n + 1)
                    for b in range(NG * (t + 1)):
                        last = pe.transpose(wk[:, 2 + b // 4, P * (b % 4):P * (b % 4) + P], sc[:, P * b:P * b + P],
                                            ident[:])
                    last.then_inc(ev["w_pturned"], 1)
                return step

            def w_pv(h, t):
                n = 2 * h + t

                def step():
                    pe.wait_ge(ev["w_pt"], n + 1)
                    if n:
                        pe.wait_ge(ev["w_o"], n)
                    for g in range(NG):
                        for kt in range(t + 1):
                            b = g * (t + 1) + kt
                            at = P * (HS * g + h)
                            last = pe.matmul(wk[:, 4, 0:P], pt[:, P * b:P * b + P], swa_v[:, kt, at:at + P],
                                             start=b == 0, stop=b == NG * (t + 1) - 1)
                    last.then_inc(ev["w_pv"], 1)
                return step

            pe.wait_ge(ev["ab_split"], 1)
            for t in range(TT):
                for k in range(KC):
                    for a, (w, v) in enumerate(((st_hi, ab_whi), (st_lo, ab_whi), (st_hi, ab_wlo))):
                        last = pe.matmul(wk[:, 5, 2 * HG * t:2 * HG * t + 2 * HG], w[:, k, P * t:P * t + P],
                                         v[:, k, :], start=k == 0 and a == 0, stop=k == KC - 1 and a == 2)
            last.then_inc(ev["ab_done"], 1)

            def ob_turn():
                pe.wait_ge(ev["w_o"], 2 * HS)
                pe.wait_ge(ev["b_xc"], 6)
                turn(lambda t, b: o_b[:, t, P * b:P * b + P], tbv, ev["d_turned"])

            def g_sums():
                pe.wait_ge(ev["ab_vec"], 7)
                pe.matmul(wk[:, 5, 0:16], tri[:], gg, start=True, stop=True)
                pe.matmul(wk[:, 5, 16:32], ones[:], gg, start=True, stop=True).then_inc(ev["g_sums"], 1)

            for gi in range(8):
                h = gi // 2
                t = gi % 2
                after = {0: w_sc(h, t), 3: w_ptr(h, t), 5: w_pv(h, t)}
                if gi == 7:
                    after[6] = ob_turn
                if gi == 1:
                    after[7] = g_sums
                if 1 <= gi <= 6:
                    after[1] = b_turn(gi - 1)
                if 2 <= gi <= 5:
                    after[4] = b_ss(gi - 2)
                group(QB + gi, GB_ + gi, 8, st_hi, st_lo, after=after)

            W = [wk[:, 2 + n, :] for n in range(4)]

            def blk(ap, b):
                return ap[:, P * b:P * b + P]

            def gdn_steps(i):
                def turn_kv():
                    pe.wait_ge(ev["n_load"], i + 1)
                    pe.wait_ge(ev["n_rb"], i + 1)
                    for b in range(4):
                        pe.transpose(blk(W[0], b), blk(kqv[:, 1, :], b), ident[:])
                    for b in range(4):
                        last = pe.transpose(blk(W[1], b), blk(kqv[:, 2, :], b), ident[:])
                    last.then_inc(ev["n_kv"], 1)
                    pe.matmul(W[2], ones[:], Tm[:].rearrange("p b t -> p (b t)"), start=True, stop=True)
                    pe.matmul(W[3], ones[:], Um[:].rearrange("p b t -> p (b t)"), start=True, stop=True)\
                        .then_inc(ev["n_rows"], 1)

                def products():
                    pe.wait_ge(ev["n_rv"], i + 1)
                    for b in range(4):
                        pe.matmul(blk(W[0], b), blk(kqv[:, 1, :], b), blk(kqv[:, 1, :], b), start=True, stop=True)
                    for b in range(4):
                        last = pe.matmul(blk(W[1], b), blk(kqv[:, 1, :], b), blk(kqv[:, 0, :], b), start=True,
                                         stop=True)
                    last.then_inc(ev["n_kk"], 1)

                def level_a(l):
                    def step():
                        pe.wait_ge(ev["n_Ls"], 6 * i + l + 1)
                        if l:
                            pe.wait_ge(ev["n_T"], 5 * i + l)
                        else:
                            pe.wait_ge(ev["n_init"], 4 * i + 4)
                        for b in range(4):
                            last = pe.matmul(blk(W[0], b), Ls[:, l % 2, b, :], Tm[:, b, :], start=True, stop=True)
                        last.then_inc(ev["n_P"], 1)
                    return step

                def level_b(l):
                    h = 2 << l

                    def half(ap, which):
                        return ap.rearrange("p (n two c) -> p n two c", two=2, c=h)[:, :, which, :]

                    def step():
                        pe.wait_ge(ev["n_Pc"], 6 * i + l + 1)
                        if l:
                            pe.wait_ge(ev["n_U"], 6 * i + l)
                        else:
                            pe.wait_ge(ev["n_aq0"], i + 1)
                        if l < LEVELS - 1:
                            for b in range(4):
                                pe.matmul(W[1][:, 64 * b:64 * b + 64], Um[:, b, :], half(Pm[:, b, :], 0),
                                          start=True, stop=True)
                        for b in range(4):
                            last = pe.matmul(W[2][:, 64 * b:64 * b + 64], Pm[:, b, :], half(Um[:, b, :], 1),
                                             start=True, stop=True)
                        last.then_inc(ev["n_TU"], 1)
                    return step

                def solve():
                    pe.wait_ge(ev["n_U"], 6 * i + 6)
                    for b in range(4):
                        last = pe.matmul(blk(W[0], b), Um[:, b, :], rv[:, b, :], start=True, stop=True)
                    last.then_inc(ev["n_u"], 1)
                    for h in range(2):
                        last = pe.matmul(blk(W[1], h), rk[:, 2 * h + 1, :], Um[:, 2 * h + 1, :], start=True, stop=True)
                    last.then_inc(ev["n_w"], 1)

                def first_chunk():
                    pe.wait_ge(ev["n_vn"], i + 1)
                    for h in range(2):
                        last = pe.matmul(blk(W[2], h), kd[:, 2 * h, :], Pm[:, 2 * h, :], start=True, stop=True)
                    last.then_inc(ev["n_S"], 1)
                    for h in range(2):
                        last = pe.matmul(blk(W[3], 2 * h), aq[:, 2 * h, :], Pm[:, 2 * h, :], start=True, stop=True)
                    last.then_inc(ev["n_o0"], 1)

                def with_state():
                    pe.wait_ge(ev["n_wT"], i + 1)
                    pe.wait_ge(ev["n_Sc"], i + 1)
                    for h in range(2):
                        last = pe.matmul(blk(W[0], h), Tm[:, h, :], state[:, h, :], start=True, stop=True)
                    last.then_inc(ev["n_ws"], 1)
                    for h in range(2):
                        last = pe.matmul(blk(W[1], h), blk(kqv[:, 0, :], 2 * h + 1), state[:, h, :], start=True,
                                         stop=True)
                    last.then_inc(ev["n_qs"], 1)

                def second_chunk():
                    pe.wait_ge(ev["n_vn1"], i + 1)
                    for h in range(2):
                        last = pe.matmul(blk(W[3], 2 * h + 1), aq[:, 2 * h + 1, :], Pm[:, 2 * h + 1, :], start=True,
                                         stop=True)
                    last.then_inc(ev["n_o1"], 1)

                mid = {7 + l: level_a(l) for l in range(LEVELS)} | {13: solve, 14: first_chunk, 15: with_state}
                after = {7 + l: level_b(l) for l in range(LEVELS)} | {2: turn_kv, 4: products, 15: second_chunk}
                return [({m - 8 * n: f for m, f in mid.items() if m // 8 == n},
                         {m - 8 * n: f for m, f in after.items() if m // 8 == n}) for n in range(2)]

            with pe.Fori(0, 4) as i:
                for n, (mid, after) in enumerate(gdn_steps(i)):
                    group(QC + n + 2 * i, GC_ + n + 2 * i, 8, st_hi, st_lo, mid=mid, after=after)

            def oa_turn():
                pe.wait_ge(ev["n_out"], 4)
                for n in range(2):
                    dst = wk[:, 2 * n:2 * n + 2, :].rearrange("p a (b t) -> p (a b) t", t=TT * P)
                    turn(lambda t, b: o_a[:, t, 4 * n + b, :], dst, ev["d_turned"])

            def m_turn(cg):
                def step():
                    pe.wait_ge(ev["m_mixed"], cg + 1)
                    pe.wait_ge(ev["d_lo"], 3 + cg)
                    turn(lambda t, b: mixed[:, t, P * b:P * b + P], tbv, ev["d_turned"])
                return step

            pe.wait_ge(ev["d_lo"], 1)
            for cg in range(4):
                group(QD, GD_ + cg, 2, ob_hi, ob_lo, i0=2 * cg, after={1: oa_turn} if cg == 1 else {})
            pe.wait_ge(ev["d_lo"], 3)
            for cg in range(4):
                group(QD, GD_ + 4 + cg, 4, oa_hi, oa_lo, i0=8 + 4 * cg, after={1: m_turn(cg - 1)} if cg else {})

            def x_turn(g):
                def step():
                    pe.wait_ge(acc_free, 2 * g + 2 * GE + 4)
                    if g:
                        pe.wait_ge(ev["e_lo"], 4 * g)
                    else:
                        pe.wait_ge(ev["d_lo"], 7)
                    turn(lambda t, b: x1[:, t, N * g + P * b:N * g + P * b + P], tbv, ev["e_turned"])
                return step

            def last_mix():
                m_turn(3)()
            def after_last_mix():
                pe.wait_ge(ev["d_lo"], 7)
            group(QE, GE, 8, mix_hi, mix_lo, after={1: last_mix, 5: after_last_mix})
            for g in range(1, 4):
                group(QE + g, GE + g, 8, mix_hi, mix_lo, after={1: x_turn(g - 1)})

            def u_turn(half, g, first=False):
                def step():
                    pe.wait_ge(ev["u_squared"], g + 8 * half + 1)
                    if first:
                        if half == 0:
                            pe.wait_ge(ev["e_lo"], 16)
                        else:
                            pe.wait_ge(ev["u_lo"], 8)
                    else:
                        pe.wait_ge(ev["u_lo"], g + 8 * half)
                    turn(lambda t, b: uq[:, t, P * b:P * b + P], tbv, ev["u_turned"])
                return step

            def wait_e():
                pe.wait_ge(ev["e_lo"], 16)

            for half, (qf, qg, gf, gg_) in enumerate(((QF0, QG0, GF0, GG0), (QF1, QG1, GF1, GG1))):
                group(qf, gf, 8, st_hi, st_lo, after={} if half else {1: x_turn(3), 5: wait_e})
                group(qf + 1, gf + 1, 8, st_hi, st_lo, after={1: u_turn(half, 0, True)})
                with pe.Fori(2, 8) as g:
                    group(qf + g, gf + g, 8, st_hi, st_lo, after={1: u_turn(half, g - 1)})

                def wait_u():
                    pe.wait_ge(ev["u_lo"], 8 * half + 8)
                group(qg, gg_, 16, u_hi, u_lo, after={1: u_turn(half, 7), 13: wait_u})
                with pe.Fori(1, 4) as g:
                    group(qg + 2 * g, gg_ + g, 16, u_hi, u_lo)

        @block.scalar
        def _(act):
            def split(q, i):
                act.wait_ge(landed[i // 2 % RAW], 16 * (q + i // 8) + 16)
                act.wait_ge(piece_used, 8 * q + i + 1)
                act.activation(hi[:, i % PIECES], raw[:, i // 2 % RAW, 2 * (i % 2):2 * (i % 2) + 2, :], ACT.Copy)\
                    .then_inc(hi_ready, 1)

            def ahead(q, n, steps={}, i0=0, last=False, read_out=()):
                for m in range(n):
                    if m in steps:
                        steps[m]()
                    if read_out and m >= n - 2:
                        read_out[m - (n - 2)]()
                    if not last or i0 + m + PIECES < n:
                        split(q, i0 + m + PIECES)

            def wait_apart(sem_, value):
                act.wait_ge(sem_, value)
                act.nop(nofuse=True)

            def f(out_, in_, func, wait, done, **kw):
                if wait is not None:
                    act.wait_ge(*wait)
                act.activation(out_, in_, func, **kw).then_inc(done, 1)

            def read_out(q, g, n, dst, func=ACT.Copy, scale=rstd1, before=None):
                def first():
                    if before is not None:
                        act.wait_ge(*before)
                    act.wait_ge(acc0_done, g + 1)
                    act.activation(dst(0), acc[:, 0], func, scale=scale[:, 0:1]).then_inc(acc_free, 1)

                def second():
                    act.wait_ge(piece_used, 8 * q + n + PIECES)
                    act.activation(dst(1), acc[:, 1], func, scale=scale[:, 1:2]).then_inc(acc_free, 1)
                return first, second

            act.preload_act_table_set("trig_and_small")
            act.wait_ge(ev["cols_made"], 1)
            for k in range(KC):
                act.wait_ge(ev["x_turned"], k // 4 + 1)
                src = wk[:, (0, 2, 4, 0)[k // 4] + k % 4 // 2, TT * P * (k % 2):TT * P * (k % 2) + TT * P]
                act.activation(st_hi[:, k], src, ACT.Copy, scale=lncol[:, k:k + 1]).then_inc(ev["x_split_hi"], 1)
                if k == 3:
                    act.wait_ge(piece_used, PIECES)
                for p in FIRST_SPLITS.get(k, ()):
                    split(0, p)
                if k == 3:
                    with nc.allow_non_contiguous_dma(reason="256 positions"):
                        act.dma_start(pos_i[:], positions.rearrange("(t p) -> p t", p=P)).then_inc(ev["pos_ready"], 16)
                    act.dma_start(invf[:], inv_freq.partition_broadcast(P)).then_inc(ev["pos_ready"], 16)
                    act.dma_start(bc[:, 0, :], q_norm_w.partition_broadcast(P)).then_inc(ev["w_bcast"], 16)
                    act.dma_start(bc[:, 1, :], k_norm_w.partition_broadcast(P)).then_inc(ev["w_bcast"], 16)
                    act.dma_start(gnw[:], gdn_norm_w.partition_broadcast(P)).then_inc(ev["w_head"], 16)
                    act.dma_start(alog_c, a_log.partition_broadcast(P)).then_inc(ev["w_head"], 16)
                    act.dma_start(dt_c, dt_bias.partition_broadcast(P)).then_inc(ev["w_head"], 16)
                    act.dma_start(ab_raw[:], w_in_v[:, :, COL_AB:COL_AB + 2 * HG]).then_inc(ev["w_ab"], 16)

            def sines():
                f(arg[:], arg[:], ACT.Sin, (ev["angles"], 13), ev["sincos"])
                act.preload_act_table_set("natural_log_exp_and_others")

            def x_sum(t):
                def step():
                    f(x_scr[:], x_tok[:, t], ACT.Square, (ev["x_square"], t) if t else None, ev["x_square"],
                      accum_out=ssx[:, t:t + 1])
                return step

            def x_factor():
                f(lnx, ssx, ACT.Ln, (ev["x_square"], 2), ev["x_square"], scale=1.0 / D, bias=EPS)
                f(rstd1, lnx, ACT.Exp, (ev["x_square"], 3), ev["x_square"], scale=-0.5)
                f(ab_whi[:], ab_raw[:], ACT.Copy, (ev["w_ab"], 16), ev["ab_hi"])
                act.wait_ge(ev["x_square"], 4)

            def a_store(which, i, n):
                def step():
                    act.wait_ge(ev["a_turned"], n + 1)
                    act.activation(swa_qk[:, which, HS * i:HS * i + HS, :], tbv, ACT.Copy)\
                        .then_inc(ev["a_stored"], 1)
                return step

            def a_group(q, n, steps={}):
                ahead(q, 8, steps, read_out=read_out(q, q, 8, lambda t: xs[:, t].rearrange("p h d -> p (h d)"),
                                                     before=(ev["a_t12"], n) if n else None))
                f(sq[:], xs[:], ACT.Square, (acc_free, 2 * q + 4), ev["a_sq"])
                f(ln8, ss8, ACT.Ln, (ev["a_ss"], n + 1), ev["a_ln"], scale=1.0 / P, bias=EPS)
                f(rs8, ln8, ACT.Exp, (ev["a_ln"], n + 1), ev["a_rs"], scale=-0.5)

            for n in range(6):
                if n == 0:
                    steps = {2: sines, 3: x_sum(0), 4: x_sum(1), 5: x_factor}
                else:
                    steps = {4: a_store((n - 1) % 2, (n - 1) // 2, n - 1)}
                a_group(QA + n, n, steps)
            for i in range(3):
                ahead(QA + 6 + i, 8, {} if i else {4: a_store(1, 2, 5)},
                      read_out=read_out(QA + 6 + i, GA_ + 6 + i, 8, lambda t, i=i: swa_v[:, t, N * i:N * i + N]))

            def w_load(h):
                def step():
                    if h:
                        act.wait_ge(ev["w_scores"], 2 * h)
                    else:
                        act.wait_ge(ev["a_stored"], 6)
                    act.activation(qc[:], swa_qk[:, 0, :, :].rearrange("p (g h) t -> p h g t", h=HS)[:, h], ACT.Copy)\
                        .then_inc(ev["w_q"], 1)
                return step

            def w_exp(h, t):
                n = 2 * h + t

                def step():
                    f(sc[:, 0:NG * (t + 1) * P], sc[:, 0:NG * (t + 1) * P], ACT.Exp, (ev["w_nm"], n + 1), ev["w_exp"],
                      scale=SCALE, bias=nm[:, t:t + 1], accum_out=sm[:, t:t + 1])
                return step

            def w_pt(h, t):
                n = 2 * h + t

                def step():
                    if n:
                        act.wait_ge(ev["w_pv"], n)
                    w = NG * (t + 1) * P
                    f(pt[:, 0:w], wk[:, 2:4, :].rearrange("p a n -> p (a n)")[:, 0:w], ACT.Copy,
                      (ev["w_pturned"], n + 1), ev["w_pt"])
                return step

            def both(*steps):
                def step():
                    for a in steps:
                        a()
                return step

            def b_xc(n):
                def step():
                    if n:
                        act.wait_ge(ev["b_conv"], 16 * n)
                    act.wait_ge(ev["pad_made"], 1)
                    f(xc[:, :, CONV - 1:CONV - 1 + TT * P], tbv, ACT.Copy, (ev["b_turned"], n + 1), ev["b_xc"])
                return step

            def b_sigmoid(n):
                e = e2[n % 2]

                def step():
                    f(e[:], e[:], ACT.Exp, (ev["b_clamp"], n + 1), ev["b_sig"], scale=-1.0)
                    f(e[:], e[:], ACT.Ln, (ev["b_sig"], 3 * n + 1), ev["b_sig"], bias=1.0)
                    f(e[:], e[:], ACT.Exp, (ev["b_sig"], 3 * n + 2), ev["b_sig"], scale=-1.0)
                return step

            def b_square(n):
                e = e2[n % 2]

                def step():
                    f(e[:], y2[n % 2][:], ACT.Square, (ev["b_silu"], n + 1), ev["b_sq"])
                return step

            def b_norm(n):
                e = e2[n % 2]

                def step():
                    f(e[:], tbv, ACT.Ln, (ev["b_ss"], n + 1), ev["b_nl"], bias=EPS)
                    f(e[:], e[:], ACT.Exp, (ev["b_nl"], n + 1), ev["b_rn"], scale=-0.5)
                return step

            def ab_chain():
                f(tmpa, tmpa, ACT.Exp, (ev["ab_vec"], 3), ev["ab_act"], scale=-1.0)
                f(tmpa, tmpa, ACT.Ln, (ev["ab_act"], 1), ev["ab_act"], bias=1.0)
                f(beta, tmpa, ACT.Exp, (ev["ab_act"], 2), ev["ab_act"], scale=-1.0)
                f(tmpc, tmpc, ACT.Exp, (ev["ab_vec"], 5), ev["ab_act"], scale=-1.0)
                f(tmpc, tmpc, ACT.Ln, (ev["ab_act"], 4), ev["ab_act"], bias=1.0)
                f(ea_c, alog_c, ACT.Exp, (ev["w_head"], 48), ev["ab_act"])

            def ob_hi_step():
                f(ob_hi[:], tbv, ACT.Copy, (ev["d_turned"], 1), ev["d_hi"])

            def g_exps():
                f(eG, Gc, ACT.Exp, (ev["g_vec"], 1), ev["g_exps"])
                f(kds, kds, ACT.Exp, (ev["g_vec"], 2), ev["g_exps"])

            w_load(0)()
            for gi in range(8):
                h = gi // 2
                n = gi - 1
                t = gi % 2
                steps = {m: [] for m in range(8)}
                if gi == 2:
                    steps[0] += [g_exps]
                if gi >= 2:
                    steps[0] += [b_sigmoid(n - 1)]
                steps[2] += [w_exp(h, t)]
                if 1 <= gi <= 6:
                    steps[2] += [b_xc(n)]
                if 2 <= gi <= 5:
                    steps[3] += [b_square(n - 1)]
                    steps[5] += [b_norm(n - 1)]
                steps[4] += [w_pt(h, t)]
                if gi == 7:
                    steps[7] += [ob_hi_step]
                if gi == 0:
                    steps[5] += [ab_chain]
                if gi == 7:
                    steps[4] += [b_sigmoid(6)]
                if t and gi < 7:
                    steps[6] += [w_load(h + 1)]
                steps = {m: both(*a) for m, a in steps.items() if a}
                if gi < 6:
                    dst, before = lambda t: stage[:, t], (ev["b_turned"], gi) if gi else None
                else:
                    dst, before = lambda t, a=4 * (gi - 6): zs[:, t, a:a + 4, :].rearrange("p h d -> p (h d)"), None
                ahead(QB + gi, 8, steps, read_out=read_out(QB + gi, GB_ + gi, 8, dst, before=before))
            b_sigmoid(7)()

            def gate(g, cnt, which, i):
                gt = gates[:, which, bass.ds(i, 1)].rearrange("p o t n -> p (o t) n")

                def exp_in():
                    wait_apart(acc_free, 2 * g + 4)
                    f(gt, gt, ACT.Exp, None, ev["c_gate"], scale=-1.0)

                def ln():
                    wait_apart(ev["c_gate"], 3 * cnt + 1)
                    f(gt, gt, ACT.Ln, None, ev["c_gate"], bias=1.0)

                def exp_out():
                    wait_apart(ev["c_gate"], 3 * cnt + 2)
                    f(gt, gt, ACT.Exp, None, ev["c_gate"], scale=-1.0)
                return exp_in, ln, exp_out

            def gdn_steps(i):
                def load():
                    act.wait_ge(ev["b_out"], 6)
                    act.wait_ge(ev["b_turned"], 6)
                    act.wait_ge(ev["w_pv"], 2 * HS)
                    f(kqv[:].rearrange("p w (h t) -> p w h t", h=2), gdn_qkv[:, :, bass.ds(2 * i, 2), :], ACT.Copy,
                      None, ev["n_load"])

                def decay():
                    f(Pm[:], Pm[:], ACT.Exp, (ev["n_min"], i + 1), ev["n_decay"])

                def copy_p(l):
                    def step():
                        if l == 0:
                            act.wait_ge(ev["n_aq0"], i + 1)
                        f(Pm[:].rearrange("p b t -> p (b t)"), wk[:, 2, :], ACT.Copy, (ev["n_P"], 6 * i + l + 1),
                          ev["n_Pc"])
                    return step

                def copy_w():
                    f(Tm[:, 0:2, :].rearrange("p b t -> p (b t)"), wk[:, 3, 0:2 * P], ACT.Copy, (ev["n_w"], i + 1),
                      ev["n_wT"])

                def copy_s():
                    f(state[:].rearrange("p b t -> p (b t)"), wk[:, 4, 0:2 * P], ACT.Copy, (ev["n_S"], i + 1),
                      ev["n_Sc"])

                def norm(gate_exp, gate_ln, gate_out):
                    gate_exp()
                    f(Ls[:, 0], LT[:], ACT.Square, (ev["n_oc"], 2 * i + 2), ev["n_sq"], scale=SCALE)
                    gate_ln()
                    f(nln, nss, ACT.Ln, (ev["n_nss"], i + 1), ev["n_nl"], bias=P * EPS)
                    f(nrs, nln, ACT.Exp, (ev["n_nl"], i + 1), ev["n_nr"], scale=-0.5)
                    gate_out()

                steps = {0: load, 2: decay, 6: copy_p(0), 8: both(copy_p(1), copy_p(2)),
                         10: both(copy_p(3), copy_p(4)), 12: both(copy_p(5), copy_w), 14: copy_s}
                return steps, norm

            with act.Fori(0, 4) as i:
                steps, norm = gdn_steps(i)
                steps |= dict(zip((9, 11, 13), gate(GC_ + 2 * i, 2 * i, 0, i)))
                ahead(QC + 2 * i, 8, {m: a for m, a in steps.items() if m < 8})
                ahead(QC + 1 + 2 * i, 8, {m - 8: a for m, a in steps.items() if m >= 8})
                norm(*gate(GC_ + 1 + 2 * i, 2 * i + 1, 1, i))

            def oa_hi_step():
                for n in range(2):
                    f(oa_hi[:, 4 * n:4 * n + 4, :], wk[:, 2 * n:2 * n + 2, :].rearrange("p a (b t) -> p (a b) t",
                                                                                        t=TT * P),
                      ACT.Copy, (ev["d_turned"], n + 2), ev["d_hi"])

            def m_hi(cg):
                def step():
                    f(mix_hi[:, 4 * cg:4 * cg + 4, :], tbv, ACT.Copy, (ev["d_turned"], 4 + cg), ev["d_hi"])
                return step

            for cg in range(4):
                ahead(QD, 2, {1: oa_hi_step} if cg == 1 else {}, i0=2 * cg)
            for cg in range(4):
                ahead(QD, 4, {1: m_hi(cg - 1)} if cg else {}, i0=8 + 4 * cg)

            def x_hi(g):
                def step():
                    act.wait_ge(ev["e_turned"], g + 1)
                    for b in range(4):
                        act.activation(st_hi[:, 4 * g + b], tbv[:, b], ACT.Copy,
                                       scale=lncol[:, KC + 4 * g + b:KC + 4 * g + b + 1]).then_inc(ev["e_hi"], 1)
                return step

            ahead(QE, 8, {1: m_hi(3)})
            for g in range(1, 4):
                ahead(QE + g, 8, {1: x_hi(g - 1)})

            def x_stats():
                act.wait_ge(acc_free, 2 * (GE + 3) + 4)
                for t in range(TT):
                    f(x_scr2[:], x1[:, t], ACT.Square, (ev["e_square"], t) if t else None, ev["e_square"],
                      accum_out=ssx2[:, t:t + 1])
                f(lnx2, ssx2, ACT.Ln, (ev["e_square"], 2), ev["e_square"], scale=1.0 / D, bias=EPS)
                f(rstd2, lnx2, ACT.Exp, (ev["e_square"], 3), ev["e_square"], scale=-0.5)
                act.wait_ge(ev["e_square"], 4)

            def u_hi_step(half, g):
                def step():
                    wait_apart(ev["u_turned"], g + 8 * half + 1)
                    f(u_hi[:, span(4 * g, 4), :], tbv, ACT.Copy, None, ev["u_hi"])
                return step

            def u_group(q, g, n, steps):
                ahead(q, 8, steps, read_out=read_out(
                    q, g, 8, lambda t: us[:, t], func=ACT.Relu, scale=rstd2,
                    before=None if n is None else (ev["u_squared"], n)))

            for half, (qf, qg, gf, gg_) in enumerate(((QF0, QG0, GF0, GG0), (QF1, QG1, GF1, GG1))):
                if half:
                    u_group(qf, gf, 8, {})
                else:
                    u_group(qf, gf, None, {1: x_hi(3), 3: x_stats})
                u_group(qf + 1, gf + 1, 1 + 8 * half, {2: u_hi_step(half, 0)})
                with act.Fori(2, 8) as g:
                    u_group(qf + g, gf + g, g + 8 * half, {2: u_hi_step(half, g - 1)})
                ahead(qg, 16, {2: u_hi_step(half, 7)})
                if half == 0:
                    with act.Fori(1, 4) as g:
                        ahead(qg + 2 * g, 16)
                else:
                    def store(g, tiles=slice(0, TT), banks=TT):
                        act.wait_ge(acc_free, 2 * (gg_ + g) + TT + banks)
                        act.dma_start(out_v[:, tiles, span(N * g, N)], x1[:, tiles, span(N * g, N)])\
                            .then_inc(ev["stored"], 16)
                    with act.Fori(1, 3) as g:
                        ahead(qg + 2 * g, 16, {2: lambda: store(g - 1)})
                    ahead(qg + 6, 16, {2: lambda: store(2)}, last=True)
                    for t in range(TT):
                        store(3, slice(t, t + 1), t + 1)
                    act.wait_ge(ev["stored"], 16 * (3 + TT))

        @block.vector
        def _(dve):
            def split(q, i):
                dve.wait_ge(hi_ready, 8 * q + i + 1)
                dve.tensor_tensor(lo[:, i % PIECES], raw[:, i // 2 % RAW, 2 * (i % 2):2 * (i % 2) + 2, :],
                                  hi[:, i % PIECES].bitcast(F32), ALU.subtract).then_inc(lo_ready, 1)

            def ahead(q, n, steps={}, i0=0, last=False, read_out=()):
                for m in range(n):
                    if m in steps:
                        steps[m]()
                    if read_out and m >= n - 2:
                        read_out[m - (n - 2)]()
                    if not last or i0 + m + PIECES < n:
                        split(q, i0 + m + PIECES)

            def tt_(out_, a, b, op, wait, done):
                if wait is not None:
                    dve.wait_ge(*wait)
                dve.tensor_tensor(out_, a, b, op).then_inc(done, 1)

            def ts_(out_, a, s1, s2, op0, op1, wait, done):
                if wait is not None:
                    dve.wait_ge(*wait)
                if s2 is None:
                    dve.tensor_scalar(out_, a, s1, None, op0).then_inc(done, 1)
                else:
                    dve.tensor_scalar(out_, a, s1, s2, op0, op1).then_inc(done, 1)

            dve.wait_ge(ev["rows_turned"], 1)
            dve.tensor_copy(lncol[:], wk[:, 4, 0:2 * KC]).then_inc(ev["cols_made"], 1)
            dve.tensor_copy(convcol[:], wk[:, 4, P:P + 96]).then_inc(ev["cols_made"], 1)
            dve.wait_ge(ev["res_product"], 1)
            for a in range(2):
                last = dve.tensor_scalar(swa_mask[:, :, a, :], wk[:, 5, 0:NG * P].rearrange("p (g k) -> p g k", g=NG),
                                         1.0, -NEG, ALU.subtract, ALU.mult)
            last.then_inc(ev["res_mask"], 1)
            for k in range(KC):
                dve.wait_ge(ev["x_split_hi"], k // 2 * 2 + 2)
                src = wk[:, (0, 2, 4, 0)[k // 4] + k % 4 // 2, TT * P * (k % 2):TT * P * (k % 2) + TT * P]
                dve.scalar_tensor_tensor(out=st_lo[:, k], in0=src, scalar=lncol[:, k:k + 1],
                                         in1=st_hi[:, k].bitcast(F32), op0=ALU.mult, op1=ALU.subtract)\
                    .then_inc(ev["x_split_lo"], 1)
                for p in FIRST_SPLITS.get(k, ()):
                    split(0, p)

            def angles():
                dve.wait_ge(ev["pos_ready"], 32)
                dve.tensor_copy(posf, pos_i[:]).then_inc(ev["angles"], 1)
                for t in range(TT):
                    ts_(arg[:, 0, t, :], invf[:], posf[:, t:t + 1], None, ALU.mult, None, (ev["angles"], 1),
                        ev["angles"])
                dve.wait_ge(ev["angles"], 3)
                dve.tensor_copy(arg[:, 1], arg[:, 0]).then_inc(ev["angles"], 1)
                magic = 1.5 * 2.0 ** 23
                for a in range(2):
                    ts_(turns[:, a], arg[:, a], 1.0 / (2 * math.pi), 0.25 * a, ALU.mult, ALU.add, (ev["angles"], 4),
                        ev["angles"])
                ts_(turns[:], turns[:], magic, None, ALU.add, None, (ev["angles"], 6), ev["angles"])
                ts_(turns[:], turns[:], magic, None, ALU.subtract, None, (ev["angles"], 7), ev["angles"])
                for n, part in enumerate(TWO_PI_PARTS):
                    dve.wait_ge(ev["angles"], 8 + n)
                    dve.scalar_tensor_tensor(out=arg[:], in0=turns[:], scalar=-part, in1=arg[:], op0=ALU.mult,
                                             op1=ALU.add).then_inc(ev["angles"], 1)
                ts_(arg[:, 1], arg[:, 1], math.pi / 2, None, ALU.add, None, (ev["angles"], 11), ev["angles"])
                pi_in = 3.1415925
                ts_(arg[:], arg[:], pi_in, -pi_in, ALU.min, ALU.max, (ev["angles"], 12), ev["angles"])

            def tables():
                dve.wait_ge(ev["sincos"], 1)
                dve.wait_ge(ev["w_bcast"], 32)
                for w in range(2):
                    for half in range(2):
                        a = slice(64 * half, 64 * half + 64)
                        other = slice(64 - 64 * half, 128 - 64 * half)
                        dve.tensor_tensor(rope_c[:, w, :, a], arg[:, 1], bcast(bc[:, w, a], 1, [P, TT, 64]),
                                          ALU.mult).then_inc(ev["table"], 1)
                        dve.scalar_tensor_tensor(out=rope_s[:, w, :, a], in0=arg[:, 0],
                                                 scalar=-1.0 if half == 0 else 1.0,
                                                 in1=bcast(bc[:, w, other], 1, [P, TT, 64]), op0=ALU.mult,
                                                 op1=ALU.mult).then_inc(ev["table"], 1)

            def ab_split():
                dve.wait_ge(ev["ab_hi"], 1)
                dve.tensor_tensor(ab_wlo[:], ab_raw[:], ab_whi[:].bitcast(F32), ALU.subtract)\
                    .then_inc(ev["ab_split"], 1)
                dve.wait_ge(ev["table"], 8)

            def a_post(w, n):
                dve.wait_ge(ev["a_sq"], n + 1)
                dve.tensor_reduce(ss8, sq[:].rearrange("p t h d -> p (t h) d"), AX_X, ALU.add).then_inc(ev["a_ss"], 1)
                if n:
                    dve.wait_ge(ev["a_turned"], n)
                tt_(t1[:], xs[:], bcast(rope_c[:, w], 2, [P, TT, HS, P]), ALU.mult, None, ev["a_t1"])
                tt_(t2[:, :, :, 0:64], xs[:, :, :, 64:128], bcast(rope_s[:, w, :, 0:64], 2, [P, TT, HS, 64]),
                    ALU.mult, None, ev["a_t2"])
                tt_(t2[:, :, :, 64:128], xs[:, :, :, 0:64], bcast(rope_s[:, w, :, 64:128], 2, [P, TT, HS, 64]),
                    ALU.mult, None, ev["a_t2"])
                dve.wait_ge(ev["a_t2"], 2 * n + 2)
                tt_(t1[:], t1[:], t2[:], ALU.add, (ev["a_t1"], n + 1), ev["a_t12"])
                dve.wait_ge(ev["a_t12"], n + 1)
                t1f = t1[:].rearrange("p t h d -> p (t h) d")
                dve.wait_ge(ev["a_rs"], n + 1)
                ts_(ln8, ss8, 1.0 / P, EPS, ALU.mult, ALU.add, None, ev["a_newton"])
                tt_(nt8, rs8, rs8, ALU.mult, None, ev["a_newton"])
                tt_(nt8, nt8, ln8, ALU.mult, (ev["a_newton"], 5 * n + 2), ev["a_newton"])
                ts_(nt8, nt8, -0.5, 1.5, ALU.mult, ALU.add, (ev["a_newton"], 5 * n + 3), ev["a_newton"])
                tt_(rs8, rs8, nt8, ALU.mult, (ev["a_newton"], 5 * n + 4), ev["a_newton"])
                tt_(t1f, t1f, bcast(rs8, 2, [P, TT * HS, P]), ALU.mult, (ev["a_newton"], 5 * n + 5), ev["a_roped"])

            for n in range(6):
                ahead(QA + n, 8, {} if n else {1: angles, 4: tables, 6: ab_split})
                a_post(n % 2, n)
            for i in range(3):
                ahead(QA + 6 + i, 8)

            dve.wait_ge(ev["a_turned"], 6)
            dve.memset(xc[:, :, 0:CONV - 1], 0.0).then_inc(ev["pad_made"], 1)

            def w_soft(h, t):
                n = 2 * h + t
                w = NG * (t + 1) * P

                def step():
                    if n:
                        dve.wait_ge(ev["w_pturned"], n)
                    dve.wait_ge(ev["swa_mask_made"], 2)
                    mask = swa_mask[:] if t else swa_mask[:, :, 1:2, :]
                    v = "p (g a k) -> p g a k"
                    tt_(sc[:, 0:w].rearrange(v, g=NG, a=t + 1),
                        wk[:, 2:4, :].rearrange("p a n -> p (a n)")[:, 0:w].rearrange(v, g=NG, a=t + 1), mask,
                        ALU.add, (ev["w_scores"], n + 1), ev["w_masked"])
                    dve.wait_ge(ev["w_masked"], n + 1)
                    dve.tensor_reduce(mx[:, t:t + 1], sc[:, 0:w], AX_X, ALU.max).then_inc(ev["w_max"], 1)
                    ts_(nm[:, t:t + 1], mx[:, t:t + 1], -SCALE, None, ALU.mult, None, (ev["w_max"], n + 1), ev["w_nm"])
                return step

            def w_out_(h, t):
                n = 2 * h + t

                def step():
                    dve.wait_ge(ev["w_exp"], n + 1)
                    dve.reciprocal(rsm[:, t:t + 1], sm[:, t:t + 1]).then_inc(ev["w_rs"], 1)
                    dve.wait_ge(ev["w_rs"], n + 1)
                    ts_(o_b[:, t, P * h:P * h + P], wk[:, 4, 0:P], rsm[:, t:t + 1], None, ALU.mult, None,
                        (ev["w_pv"], n + 1), ev["w_o"])
                return step

            def b_conv(n, j):
                y, e = y2[n % 2], e2[n % 2]

                def step():
                    if j == 0:
                        dve.wait_ge(ev["b_xc"], n + 1)
                        if n >= 2:
                            dve.wait_ge(ev["b_out"], n - 1)
                    for b in range(4):
                        c = 3 * HG * j + 4 * n + b
                        src = xc[:, b, j:j + TT * P]
                        if j == 0:
                            dve.tensor_scalar(y[:, b], src, convcol[:, c:c + 1], None, ALU.mult)\
                                .then_inc(ev["b_conv"], 1)
                        else:
                            dve.wait_ge(ev["b_conv"], 16 * n + 4 * j + b - 3)
                            dve.scalar_tensor_tensor(out=y[:, b], in0=src, scalar=convcol[:, c:c + 1], in1=y[:, b],
                                                     op0=ALU.mult, op1=ALU.add).then_inc(ev["b_conv"], 1)
                    if j == CONV - 1:
                        ts_(e[:], y[:], SIG_MIN, None, ALU.max, None, (ev["b_conv"], 16 * n + 16), ev["b_clamp"])
                return step

            def b_silu(n):
                y, e = y2[n % 2], e2[n % 2]

                def step():
                    if n < 4:
                        tt_(y[:], y[:], e[:], ALU.mult, (ev["b_sig"], 3 * n + 3), ev["b_silu"])
                    else:
                        tt_(gdn_qkv[:, 2, 4 * (n - 4):4 * (n - 4) + 4, :], y[:], e[:], ALU.mult,
                            (ev["b_sig"], 3 * n + 3), ev["b_out"])
                return step

            def b_scaled(n):
                y, e = y2[n % 2], e2[n % 2]

                def step():
                    tt_(gdn_qkv[:, n // 2, 4 * (n % 2):4 * (n % 2) + 4, :], y[:], e[:], ALU.mult,
                        (ev["b_rn"], n + 1), ev["b_out"])
                return step

            def z_part(n):
                return zs[:, :, 4 * (n - 6):4 * (n - 6) + 4, :]

            def z_clamp(n):
                def step():
                    dve.wait_ge(acc_free, 2 * (GB_ + n) + 4)
                    ts_(e2[n % 2][:].rearrange("p b t -> p (b t)").rearrange("p (a n) -> p a n", a=TT),
                        z_part(n).rearrange("p t h d -> p t (h d)"), SIG_MIN, None, ALU.max, None,
                        (ev["b_out"], 6), ev["b_clamp"])
                    dve.wait_ge(ev["b_clamp"], n + 1)
                    tt_(z_part(n), z_part(n), gnw[:].unsqueeze(1).unsqueeze(1).to_broadcast([P, TT, 4, P]), ALU.mult,
                        (ev["w_head"], 48), ev["b_z"])
                return step

            def z_out(n):
                def step():
                    v = z_part(n).rearrange("p t h d -> p t (h d)")
                    sig = e2[n % 2][:].rearrange("p b t -> p (b t)").rearrange("p (a n) -> p a n", a=TT)
                    dve.wait_ge(ev["b_z"], 2 * (n - 6) + 1)
                    tt_(v, v, sig, ALU.mult, (ev["b_sig"], 3 * n + 3), ev["b_z"])
                return step

            def by_head(ap):
                return ap.rearrange("p (h t) -> p t h", t=TT)

            def ab_chain():
                dve.wait_ge(ev["ab_done"], 1)
                dve.wait_ge(ev["w_head"], 48)
                for t in range(TT):
                    ts_(ab_s[:, t], wk[:, 5, 16 * t:16 * t + 16], rstd1[:, t:t + 1], None, ALU.mult, None, None,
                        ev["ab_vec"])
                ts_(by_head(tmpa), ab_s[:, :, HG:2 * HG], SIG_MIN, None, ALU.max, None, (ev["ab_vec"], 2), ev["ab_vec"])
                tt_(by_head(tmpb), ab_s[:, :, 0:HG], bcast(dt_c, 1, [P, TT, HG]), ALU.add, None, ev["ab_vec"])
                dve.wait_ge(ev["ab_vec"], 4)
                dve.scalar_tensor_tensor(out=tmpc, in0=tmpb, scalar=-1.0, in1=tmpb, op0=ALU.mult, op1=ALU.max)\
                    .then_inc(ev["ab_vec"], 1)
                dve.wait_ge(ev["ab_act"], 5)
                dve.scalar_tensor_tensor(out=tmpc, in0=tmpb, scalar=0.0, in1=tmpc, op0=ALU.max, op1=ALU.add)\
                    .then_inc(ev["ab_vec"], 1)
                dve.wait_ge(ev["ab_act"], 6)
                dve.wait_ge(ev["ab_vec"], 6)
                dve.scalar_tensor_tensor(out=by_head(gg), in0=by_head(tmpc), scalar=-1.0,
                                         in1=bcast(ea_c, 1, [P, TT, HG]), op0=ALU.mult, op1=ALU.mult)\
                    .then_inc(ev["ab_vec"], 1)

            def ob_lo_step():
                tt_(ob_lo[:], tbv, ob_hi[:].bitcast(F32), ALU.subtract, (ev["d_hi"], 1), ev["d_lo"])

            def g_consts():
                dve.wait_ge(ev["g_sums"], 1)
                dve.tensor_copy(Gc, wk[:, 5, 0:16]).then_inc(ev["g_vec"], 1)
                tt_(kds, wk[:, 5, 16:32], Gc, ALU.subtract, (ev["g_vec"], 1), ev["g_vec"])
                tt_(beG, beta, eG, ALU.mult, (ev["g_exps"], 1), ev["g_vec"])

            def both(*steps):
                def step():
                    for a in steps:
                        a()
                return step

            for gi in range(8):
                h = gi // 2
                n = gi - 1
                t = gi % 2
                steps = {m: [] for m in range(8)}
                if gi == 2:
                    steps[0] += [g_consts]
                steps[1] += [w_soft(h, t)]
                if gi >= 2:
                    steps[2] += [b_silu(n - 1)]
                if 1 <= gi <= 6:
                    for j in range(CONV):
                        steps[3 + j] += [b_conv(n, j)]
                if gi == 7:
                    steps[3] += [z_clamp(6)]
                    steps[5] += [z_out(6)]
                    steps[7] += [ob_lo_step]
                if gi == 0:
                    steps[5] += [ab_chain]
                steps[6] += [w_out_(h, t)]
                if 2 <= gi <= 5:
                    steps[7] += [b_scaled(n - 1)]
                steps = {m: both(*a) for m, a in steps.items() if a}
                ahead(QB + gi, 8, steps)
            z_clamp(7)()
            z_out(7)()
            dve.wait_ge(ev["b_z"], 4)

            def gate(q, g, which, i):
                gt = gates[:, which, bass.ds(i, 1)].rearrange("p o t n -> p (o t) n")

                def first():
                    dve.wait_ge(acc0_done, g + 1)
                    dve.tensor_scalar(gt[:, 0], acc[:, 0], rstd1[:, 0:1], SIG_MIN, ALU.mult, ALU.max)\
                        .then_inc(acc_free, 1)

                def second():
                    dve.wait_ge(piece_used, 8 * q + 8 + PIECES)
                    dve.tensor_scalar(gt[:, 1], acc[:, 1], rstd1[:, 1:2], SIG_MIN, ALU.mult, ALU.max)\
                        .then_inc(acc_free, 1)
                return first, second

            def flat(ap):
                return ap.rearrange("p b t -> p (b t)")

            def gdn_steps(i):
                def cols(ap):
                    return bcast(ap[:, bass.ds(4 * i, 4)], 2, [P, 4, P])

                def rows_in():
                    dve.wait_ge(ev["w_pv"], 2 * HS)
                    tt_(Tm[:], bcast(tri[:], 1, [P, 4, P]), cols(gg), ALU.mult, (ev["g_vec"], 3), ev["n_rg"])
                    tt_(Um[:], bcast(ident[:], 1, [P, 4, P]), cols(beta), ALU.mult, None, ev["n_rb"])

                def w(n):
                    return wk[:, 2 + n, :].rearrange("p (b t) -> p b t", t=P)

                def factors():
                    tt_(rk[:], w(0), cols(beG), ALU.mult, (ev["n_kv"], i + 1), ev["n_rk"])
                    tt_(kd[:], w(0), cols(kds), ALU.mult, (ev["g_exps"], 2), ev["n_kd"])
                    tt_(rv[:], w(1), cols(beta), ALU.mult, None, ev["n_rv"])
                    tt_(Pm[:], w(2), cols(Gc), ALU.subtract, (ev["n_rows"], i + 1), ev["n_diff"])
                    ts_(Pm[:], Pm[:], 0.0, None, ALU.min, None, (ev["n_diff"], i + 1), ev["n_min"])

                def system():
                    dve.wait_ge(ev["n_decay"], i + 1)
                    tt_(LT[:], w(0), Pm[:], ALU.mult, (ev["n_kk"], i + 1), ev["n_lt0"])
                    tt_(LT[:], w(3), LT[:], ALU.mult, (ev["n_lt0"], i + 1), ev["n_LT"])
                    dve.wait_ge(ev["gdn_mask_made"], 1 + 3 * (LEVELS + 1))
                    tt_(Um[:], LT[:], bcast(lmask[:, 0, :], 1, [P, 4, P]), ALU.mult, (ev["n_LT"], i + 1), ev["n_init"])
                    dve.wait_ge(ev["n_init"], 4 * i + 1)
                    dve.transpose(flat(Tm[:]), flat(Um[:])).then_inc(ev["n_init"], 1)
                    tt_(Tm[:], bcast(ident[:], 1, [P, 4, P]), Tm[:], ALU.subtract, (ev["n_init"], 4 * i + 2),
                        ev["n_init"])
                    tt_(Um[:], bcast(ident[:], 1, [P, 4, P]), Um[:], ALU.subtract, None, ev["n_init"])

                def query_keys():
                    tt_(aq[:], w(1), Pm[:], ALU.mult, (ev["n_kk"], i + 1), ev["n_aq0"])
                    tt_(aq[:], aq[:], bcast(tri[:], 1, [P, 4, P]), ALU.mult, (ev["n_aq0"], i + 1), ev["n_aq"])

                def level(l):
                    h = 2 << l

                    def half(ap, which):
                        return flat(ap).rearrange("p (n two c) -> p n two c", two=2, c=h)[:, :, which, :]

                    def step():
                        dve.wait_ge(ev["n_TU"], 6 * i + l + 1)
                        if l < LEVELS - 1:
                            v = half(Tm[:], 0)
                            tt_(v, v, wk[:, 3, 0:256].rearrange("p (n c) -> p n c", c=h), ALU.subtract,
                                (ev["n_T"], 5 * i + l) if l else (ev["n_init"], 4 * i + 4), ev["n_T"])
                        v = half(Um[:], 1)
                        tt_(v, v, wk[:, 4, 0:256].rearrange("p (n c) -> p n c", c=h), ALU.subtract,
                            (ev["n_U"], 6 * i + l) if l else (ev["n_init"], 4 * i + 4), ev["n_U"])
                    return step

                def copy_u():
                    dve.wait_ge(ev["n_u"], i + 1)
                    dve.tensor_copy(flat(Pm[:]), wk[:, 2, :]).then_inc(ev["n_vn"], 1)

                def second(ap):
                    return ap.rearrange("p (h c) d -> p h c d", c=2)[:, :, 1, :]

                def first_(ap):
                    return ap.rearrange("p (h c) d -> p h c d", c=2)[:, :, 0, :]

                def less_state():
                    dve.wait_ge(ev["n_vn"], i + 1)
                    v = second(Pm[:])
                    tt_(v, v, wk[:, 2, 0:2 * P].rearrange("p (h d) -> p h d", h=2), ALU.subtract, (ev["n_ws"], i + 1),
                        ev["n_vn1"])
                    g2 = eG[:, bass.ds(4 * i, 4)].rearrange("p (h c) -> p h c", c=2)[:, :, 1:2].to_broadcast([P, 2, P])
                    tt_(rk[:, 0:2, :], wk[:, 3, 0:2 * P].rearrange("p (h d) -> p h d", h=2), g2, ALU.mult,
                        (ev["n_qs"], i + 1), ev["n_qe"])

                def output():
                    dve.wait_ge(ev["n_o1"], i + 1)
                    dve.tensor_copy(first_(LT[:]), first_(w(3))).then_inc(ev["n_oc"], 1)
                    tt_(second(LT[:]), second(w(3)), rk[:, 0:2, :], ALU.add, (ev["n_qe"], i + 1), ev["n_oc"])
                    dve.wait_ge(ev["n_sq"], i + 1)
                    dve.tensor_reduce(nss, Ls[:, 0], AX_X, ALU.add).then_inc(ev["n_nss"], 1)
                    tt_(LT[:], LT[:], bcast(nrs, 2, [P, 4, P]), ALU.mult, (ev["n_nr"], i + 1), ev["n_on"])

                    def heads(ap):
                        return ap[:, :, bass.ds(2 * i, 2), :].rearrange("p t h d -> p h t d")
                    dve.wait_ge(ev["n_on"], i + 1)
                    tt_(heads(o_a), LT[:].rearrange("p (h c) d -> p h c d", c=2), heads(zs), ALU.mult, None,
                        ev["n_out"])

                steps = {0: rows_in, 2: factors, 4: system, 5: query_keys, 12: both(level(5), copy_u), 15: less_state}
                steps |= {7 + l: level(l) for l in range(LEVELS - 1)}
                return steps, output

            with dve.Fori(0, 4) as i:
                steps, output = gdn_steps(i)
                ahead(QC + 2 * i, 8, {m: a for m, a in steps.items() if m < 8},
                      read_out=gate(QC + 2 * i, GC_ + 2 * i, 0, i))
                ahead(QC + 1 + 2 * i, 8, {m - 8: a for m, a in steps.items() if m >= 8},
                      read_out=gate(QC + 1 + 2 * i, GC_ + 1 + 2 * i, 1, i))
                output()

            def oa_lo_step():
                for n in range(2):
                    tt_(oa_lo[:, 4 * n:4 * n + 4, :],
                        wk[:, 2 * n:2 * n + 2, :].rearrange("p a (b t) -> p (a b) t", t=TT * P),
                        oa_hi[:, 4 * n:4 * n + 4, :].bitcast(F32), ALU.subtract, (ev["d_hi"], n + 2), ev["d_lo"])

            def m_lo(cg):
                def step():
                    tt_(mix_lo[:, 4 * cg:4 * cg + 4, :], tbv, mix_hi[:, 4 * cg:4 * cg + 4, :].bitcast(F32),
                        ALU.subtract, (ev["d_hi"], 4 + cg), ev["d_lo"])
                return step

            def gated(g, pieces, dst, gate, wait):
                def first():
                    if wait is not None:
                        dve.wait_ge(*wait)
                    dve.wait_ge(acc0_done, g + 1)
                    dve.tensor_tensor(dst[:, 0], acc[:, 0], gate[:, 0, :], ALU.mult).then_inc(acc_free, 1)

                def second():
                    dve.wait_ge(piece_used, 8 * QD + pieces + PIECES)
                    dve.tensor_tensor(dst[:, 1], acc[:, 1], gate[:, 1, :], ALU.mult).then_inc(acc_free, 1)
                return first, second

            for cg in range(4):
                ahead(QD, 2, {1: oa_lo_step} if cg == 1 else {}, i0=2 * cg,
                      read_out=gated(GD_ + cg, 2 * cg + 2, part_b[:, cg], gates[:, 1, cg],
                                     (ev["c_gate"], 6 * cg + 6)))
            for cg in range(4):
                g = GD_ + 4 + cg
                ahead(QD, 4, {1: m_lo(cg - 1)} if cg else {}, i0=8 + 4 * cg,
                      read_out=gated(g, 12 + 4 * cg, mixed, gates[:, 0, cg],
                                     (ev["d_turned"], 3 + cg) if cg else None))
                dve.wait_ge(acc_free, 2 * g + 4)
                dve.tensor_tensor(mixed[:], mixed[:], part_b[:, cg], ALU.add).then_inc(ev["m_mixed"], 1)

            def x_lo(g):
                def step():
                    for b in range(4):
                        k = 4 * g + b
                        dve.wait_ge(ev["e_hi"], 4 * g + b // 2 * 2 + 2)
                        dve.scalar_tensor_tensor(out=st_lo[:, k], in0=tbv[:, b], scalar=lncol[:, KC + k:KC + k + 1],
                                                 in1=st_hi[:, k].bitcast(F32), op0=ALU.mult, op1=ALU.subtract)\
                            .then_inc(ev["e_lo"], 1)
                return step

            def add(q, g, n, cols):
                def first():
                    dve.wait_ge(ev["x_back"], 16)
                    dve.wait_ge(acc0_done, g + 1)
                    dve.tensor_tensor(x1[:, 0, cols], acc[:, 0], x1[:, 0, cols], ALU.add).then_inc(acc_free, 1)

                def second():
                    dve.wait_ge(piece_used, 8 * q + n + PIECES)
                    dve.tensor_tensor(x1[:, 1, cols], acc[:, 1], x1[:, 1, cols], ALU.add).then_inc(acc_free, 1)
                return first, second

            for g in range(4):
                ahead(QE + g, 8, {1: x_lo(g - 1) if g else m_lo(3)}, read_out=add(QE + g, GE + g, 8, span(N * g, N)))

            def u_lo_step(half, g):
                def step():
                    a = span(4 * g, 4)
                    tt_(u_lo[:, a, :], tbv, u_hi[:, a, :].bitcast(F32), ALU.subtract, (ev["u_hi"], g + 8 * half + 1),
                        ev["u_lo"])
                return step

            def u_square(g, n, first=False):
                dve.wait_ge(acc_free, 2 * g + 4)
                if not first:
                    dve.wait_ge(ev["u_turned"], n)
                dve.tensor_tensor(uq[:], us[:], us[:], ALU.mult).then_inc(ev["u_squared"], 1)

            for half, (qf, qg, gf, gg_) in enumerate(((QF0, QG0, GF0, GG0), (QF1, QG1, GF1, GG1))):
                ahead(qf, 8, {} if half else {1: x_lo(3)})
                u_square(gf, 8 * half, first=half == 0)
                ahead(qf + 1, 8, {2: u_lo_step(half, 0)})
                u_square(gf + 1, 1 + 8 * half)
                with dve.Fori(2, 8) as g:
                    ahead(qf + g, 8, {2: u_lo_step(half, g - 1)})
                    u_square(gf + g, g + 8 * half)
                ahead(qg, 16, {2: u_lo_step(half, 7)}, read_out=add(qg, gg_, 16, span(0, N)))
                with dve.Fori(1, 4 - half) as g:
                    ahead(qg + 2 * g, 16, read_out=add(qg + 2 * g, gg_ + g, 16, span(N * g, N)))
                if half:
                    ahead(qg + 6, 16, last=True, read_out=add(qg + 6, gg_ + 3, 16, span(3 * N, N)))


def kernel(**inputs):
    import concourse.bacc as bacc
    from concourse.bass_utils import run_bass_kernel_spmd

    nc = bacc.Bacc("TRN2", target_bir_lowering=False, num_devices=1,
                   dynamic_dma_scratch_size=1024)
    half = P // 2
    arrays = {
        "x": inputs["x"][0], "positions": inputs["positions"][0],
        "inv_freq": np.power(np.float32(10000.0), -np.arange(half, dtype=np.float32) / np.float32(half)),
        "ln1_w": inputs["ln1_w"][0], "w_in": inputs["w_in"][0], "conv_w": inputs["gdn_conv_w"][0],
        "a_log": inputs["gdn_a_log"][0], "dt_bias": inputs["gdn_dt_bias"][0], "gdn_norm_w": inputs["gdn_norm_w"][0],
        "w_gdn_proj": inputs["w_gdn_proj"][0], "q_norm_w": inputs["swa_q_norm_w"][0],
        "k_norm_w": inputs["swa_k_norm_w"][0], "w_swa_proj": inputs["w_swa_proj"][0], "w_out": inputs["w_out"][0],
        "ln2_w": inputs["ln2_w"][0], "w_ff1": inputs["w_ff1"][0], "w_ff2": inputs["w_ff2"][0],
    }
    arrays = {f"in_{n}": np.ascontiguousarray(a) for n, a in arrays.items()}
    args = [nc.dram_tensor(n, a.shape, mybir.dt.from_np(a.dtype), kind="ExternalInput").ap()
            for n, a in arrays.items()]
    out = nc.dram_tensor("out_x", (TT * P, D), F32, kind="ExternalOutput").ap()
    build_block(nc, *args, out)
    r = run_bass_kernel_spmd(nc, [arrays], core_ids=[0])
    return r.results[0]["out_x"].reshape(1, TT * P, D)
```
